# Optimizing a Trainium2 kernel written in Bass

```python
import math
import jax
import jax.numpy as jnp
from jax import lax
import numpy as np

D_MODEL = 1024
BATCH = 1
SEQ = 128
DEPTH = 1
DEC_BATCH = 1
DEC_SEQ = 256
PAST_LEN = 128

GRID_W = 64
EPS = 1e-6
N_MOD = 6
A_HEADS = 8
A_HEAD_DIM = 64
A_V_DIM = 2 * A_HEAD_DIM
A_QK_W = A_HEADS * 2 * A_HEAD_DIM
A_V_W = A_HEADS * A_V_DIM
Q_BLOCK = 128
ROPE_BASE = 10000.0
S_INNER = 2 * D_MODEL
S_HEADDIM = 64
S_HEADS = S_INNER // S_HEADDIM
S_GROUPS = 4
S_HPG = S_HEADS // S_GROUPS
S_STATE = 128
S_CONV = 3
S_CHUNK = 128
S_CONV_CH = S_INNER + 2 * S_GROUPS * S_STATE
N_EXPERTS = 16
EC_FACTOR = 2
D_FF = 2 * D_MODEL
IN_SIZES = (A_QK_W, A_QK_W, A_V_W, S_INNER, S_CONV_CH, 2 * S_HEADS, 2 * D_MODEL)
IN_SPLIT = tuple(sum(IN_SIZES[:i + 1]) for i in range(len(IN_SIZES) - 1))
IN_WIDTH = sum(IN_SIZES)

kernel_name = 'hybrid_diffattn_ssd_ec_diffusion_step'

def rmsnorm(x, w):
    xf = x.astype(jnp.float32)
    xf = xf * lax.rsqrt(jnp.mean(xf * xf, axis=-1, keepdims=True) + EPS)
    return (xf * w.astype(jnp.float32)).astype(x.dtype)

def axial_rope(x):
    n = x.shape[1]
    rows = n // GRID_W
    row = jnp.repeat(jnp.arange(rows), GRID_W)
    col = jnp.tile(jnp.arange(GRID_W), rows)
    pos = jnp.stack([row, col], axis=-1).astype(jnp.float32)
    half = A_HEAD_DIM // 2
    nf = half // 2
    inv_freq = jnp.power(ROPE_BASE, -jnp.arange(nf, dtype=jnp.float32) / nf)
    ang = pos[:, :, None] * inv_freq
    cos = jnp.cos(ang)[None, :, None, None].astype(x.dtype)
    sin = jnp.sin(ang)[None, :, None, None].astype(x.dtype)
    xr = x.reshape(x.shape[:-1] + (2, half))
    x1, x2 = xr[..., :nf], xr[..., nf:]
    out = jnp.concatenate([x1 * cos - x2 * sin, x2 * cos + x1 * sin], axis=-1)
    return out.reshape(x.shape)

def diff_attention(q, k, v, lam, lam_init, w_subln):
    b, nq = q.shape[:2]
    nblk = nq // Q_BLOCK
    scale = A_HEAD_DIM ** -0.5
    qb = q.reshape(b, nblk, Q_BLOCK, A_HEADS, 2, A_HEAD_DIM).transpose(1, 0, 2, 3, 4, 5)

    def block(qi):
        s = jnp.einsum('bqhmd,bkhmd->bhmqk', qi, k).astype(jnp.float32) * scale
        pr = jax.nn.softmax(s, axis=-1)
        a = pr[:, :, 0] - lam * pr[:, :, 1]
        return jnp.einsum('bhqk,bkhe->bqhe', a.astype(v.dtype), v)

    o = lax.map(block, qb)
    o = o.transpose(1, 0, 2, 3, 4).reshape(b, nq, A_HEADS, A_V_DIM)
    o = rmsnorm(o, w_subln) * (1.0 - lam_init)
    return o.reshape(b, nq, A_V_W)

def dwconv_centred(x, w, bias):
    y = lax.conv_general_dilated(
        x, w[:, None, :].astype(x.dtype), window_strides=(1,),
        padding=[((S_CONV - 1) // 2, S_CONV // 2)],
        dimension_numbers=('NWC', 'WIO', 'NWC'), feature_group_count=x.shape[-1])
    return y + bias.astype(x.dtype)

def segsum_exp(a):
    l = a.shape[-1]
    cs = jnp.cumsum(a, axis=-1)
    diff = cs[..., :, None] - cs[..., None, :]
    mask = jnp.tril(jnp.ones((l, l), dtype=bool))
    return jnp.where(mask, jnp.exp(jnp.where(mask, diff, 0.0)), 0.0)

def ssd_scan(x, dt, a, bm, cm, h0):
    b, n = x.shape[:2]
    nc = n // S_CHUNK
    f32 = jnp.float32
    xdt = (x.astype(f32) * dt[..., None]).reshape(b, nc, S_CHUNK, S_GROUPS, S_HPG, S_HEADDIM)
    bc = bm.astype(f32).reshape(b, nc, S_CHUNK, S_GROUPS, S_STATE)
    cc = cm.astype(f32).reshape(b, nc, S_CHUNK, S_GROUPS, S_STATE)
    da = (dt * a).reshape(b, nc, S_CHUNK, S_GROUPS, S_HPG).transpose(0, 3, 4, 1, 2)
    a_cs = jnp.cumsum(da, axis=-1)
    lmat = segsum_exp(da)
    cb = jnp.einsum('bclgn,bcsgn->bcgls', cc, bc)
    y_diag = jnp.einsum('bcgls,bghcls,bcsghp->bclghp', cb, lmat, xdt)
    decay_states = jnp.exp(a_cs[..., -1:] - a_cs)
    states = jnp.einsum('bclgn,bghcl,bclghp->bcghpn', bc, decay_states, xdt)
    states = jnp.concatenate([h0.astype(f32)[:, None], states], axis=1)
    chunk_tot = jnp.pad(a_cs[..., -1], ((0, 0), (0, 0), (0, 0), (1, 0)))
    decay_chunk = segsum_exp(chunk_tot)
    new_states = jnp.einsum('bghzc,bcghpn->bzghpn', decay_chunk, states)
    states_in, final = new_states[:, :-1], new_states[:, -1]
    y_off = jnp.einsum('bclgn,bcghpn,bghcl->bclghp', cc, states_in, jnp.exp(a_cs))
    y = (y_diag + y_off).reshape(b, n, S_GROUPS, S_HPG, S_HEADDIM)
    return y, final

def ssd_branch(z, xbc, dt_raw, p, h0_f, h0_b):
    b, n, _ = z.shape
    f32 = jnp.float32
    xbc = jax.nn.silu(dwconv_centred(xbc, p['conv_w'], p['conv_b']))
    xs, bm, cm = jnp.split(xbc, (S_INNER, S_INNER + S_GROUPS * S_STATE), axis=-1)
    xs = xs.reshape(b, n, S_GROUPS, S_HPG, S_HEADDIM)
    bm = bm.reshape(b, n, S_GROUPS, S_STATE)
    cm = cm.reshape(b, n, S_GROUPS, S_STATE)
    dt = jax.nn.softplus(dt_raw.astype(f32).reshape(b, n, 2, S_GROUPS, S_HPG)
                         + p['dt_bias'].astype(f32).reshape(2, S_GROUPS, S_HPG))
    a = -jnp.exp(p['a_log'].astype(f32)).reshape(2, S_GROUPS, S_HPG)
    y_f, s_f = ssd_scan(xs, dt[:, :, 0], a[0], bm, cm, h0_f)
    y_b, s_b = ssd_scan(xs[:, ::-1], dt[:, ::-1, 1], a[1], bm[:, ::-1], cm[:, ::-1], h0_b)
    y = y_f + y_b[:, ::-1] + xs.astype(f32) * p['d_skip'].astype(f32).reshape(S_GROUPS, S_HPG, 1)
    y = y.reshape(b, n, S_GROUPS, S_INNER // S_GROUPS) * jax.nn.silu(z.astype(f32)).reshape(b, n, S_GROUPS, S_INNER // S_GROUPS)
    y = rmsnorm(y, p['w_ssd_norm'].reshape(S_GROUPS, S_INNER // S_GROUPS))
    return y.reshape(b, n, S_INNER).astype(z.dtype), s_f, s_b

def token_mixer(h, p, layer_idx, ctx):
    b, n, _ = h.shape
    q, k, v, z, xbc, dt_raw, g = jnp.split(h @ p['w_in'], IN_SPLIT, axis=-1)
    q = q.reshape(b, n, A_HEADS, 2, A_HEAD_DIM)
    k = k.reshape(b, n, A_HEADS, 2, A_HEAD_DIM)
    v = v.reshape(b, n, A_HEADS, A_V_DIM)
    lam_init = 0.8 - 0.6 * math.exp(-0.3 * layer_idx)
    lam = (jnp.exp(jnp.sum(p['lam_q1'] * p['lam_k1']).astype(jnp.float32))
           - jnp.exp(jnp.sum(p['lam_q2'] * p['lam_k2']).astype(jnp.float32)) + lam_init)
    if ctx is None:
        k_all, v_all = k, v
        h0_f = jnp.zeros((b, S_GROUPS, S_HPG, S_HEADDIM, S_STATE), jnp.float32)
        h0_b = h0_f
    else:
        k_ctx, v_ctx, st_ctx = ctx
        q, k = axial_rope(q), axial_rope(k)
        k_all = jnp.concatenate([k_ctx.reshape(b, -1, A_HEADS, 2, A_HEAD_DIM).astype(k.dtype), k], axis=1)
        v_all = jnp.concatenate([v_ctx.astype(v.dtype), v], axis=1)
        st = st_ctx.astype(jnp.float32).reshape(b, 2, S_GROUPS, S_HPG, S_HEADDIM, S_STATE)
        h0_f, h0_b = st[:, 0], st[:, 1]
    o_attn = diff_attention(q, k_all, v_all, lam, lam_init, p['w_subln'])
    o_ssd, s_f, s_b = ssd_branch(z, xbc, dt_raw, p, h0_f, h0_b)
    g_attn, g_ssd = jnp.split(jax.nn.sigmoid(g), 2, axis=-1)
    merged = g_attn * (o_attn @ p['w_o_attn']) + g_ssd * (o_ssd @ p['w_o_ssd'])
    y = merged @ p['w_out']
    if ctx is None:
        new_ctx = (k.reshape(b, n, A_HEADS, 2 * A_HEAD_DIM), v,
                   jnp.stack([s_f, s_b], axis=1).reshape(b, 2, S_HEADS, S_HEADDIM, S_STATE))
    else:
        new_ctx = None
    return y, new_ctx

def expert_choice_ffn(h, w_router, w_gate, w_up, w_down):
    b, n, d = h.shape
    ntok = b * n
    cap = EC_FACTOR * ntok // N_EXPERTS
    xf = h.reshape(ntok, d)
    aff = jax.nn.softmax((xf @ w_router).astype(jnp.float32), axis=-1)
    gates, idx = lax.top_k(aff.T, cap)
    xe = xf[idx]
    he = jax.nn.silu(jnp.einsum('ecd,edf->ecf', xe, w_gate)) * jnp.einsum('ecd,edf->ecf', xe, w_up)
    ye = jnp.einsum('ecf,efd->ecd', he, w_down) * gates[..., None].astype(xe.dtype)
    out = jnp.zeros_like(xf).at[idx.reshape(-1)].add(ye.reshape(-1, d).astype(xf.dtype))
    return out.reshape(b, n, d)

def trunk_layer(x, cond, p, layer_idx, ctx):
    mod = jax.nn.silu(cond) @ p['w_ada'] + p['b_ada']
    sh1, sc1, g1, sh2, sc2, g2 = [m[:, None, :] for m in jnp.split(mod, N_MOD, axis=-1)]
    h = rmsnorm(x, p['g_pre_mix']) * (1 + sc1) + sh1
    y, new_ctx = token_mixer(h, p, layer_idx, ctx)
    x = x + g1 * rmsnorm(y, p['g_post_mix'])
    h = rmsnorm(x, p['g_pre_ffn']) * (1 + sc2) + sh2
    y = expert_choice_ffn(h, p['w_router'], p['w_gate'], p['w_up'], p['w_down'])
    x = x + g2 * rmsnorm(y, p['g_post_ffn'])
    return x, new_ctx

def setup_inputs(seed: int = 0) -> dict:
    key = jax.random.key(seed)
    ks = jax.random.split(key, 40)
    f32 = jnp.float32
    L = DEPTH

    def nrm(k, shape, s):
        return jax.random.normal(k, shape, f32) * s

    def gain(k, shape):
        return 1.0 + 0.02 * jax.random.normal(k, shape, f32)

    dt0 = jnp.exp(jax.random.uniform(ks[20], (L, 2, S_HEADS), f32, math.log(1e-3), math.log(1e-1)))
    return {
        'x_prompt': nrm(ks[0], (BATCH, SEQ, D_MODEL), 1.0),
        'x_sample': nrm(ks[1], (DEC_BATCH, DEC_SEQ, D_MODEL), 1.0),
        'cache_k': nrm(ks[2], (DEC_BATCH, L, PAST_LEN, A_HEADS, 2 * A_HEAD_DIM), 1.0),
        'cache_v': nrm(ks[3], (DEC_BATCH, L, PAST_LEN, A_HEADS, A_V_DIM), 1.0),
        'state_ssd': nrm(ks[4], (DEC_BATCH, L, 2, S_HEADS, S_HEADDIM, S_STATE), 0.5),
        'c': nrm(ks[5], (DEC_BATCH, D_MODEL), 1.0),
        'c_ctx': nrm(ks[6], (D_MODEL,), 1.0),
        'w_ada': nrm(ks[7], (L, D_MODEL, N_MOD * D_MODEL), 0.5 * D_MODEL ** -0.5),
        'b_ada': nrm(ks[8], (L, N_MOD * D_MODEL), 0.02),
        'g_pre_mix': gain(ks[9], (L, D_MODEL)),
        'g_post_mix': gain(ks[10], (L, D_MODEL)),
        'g_pre_ffn': gain(ks[11], (L, D_MODEL)),
        'g_post_ffn': gain(ks[12], (L, D_MODEL)),
        'w_in': nrm(ks[13], (L, D_MODEL, IN_WIDTH), D_MODEL ** -0.5),
        'lam_q1': nrm(ks[14], (L, A_HEAD_DIM), 0.1),
        'lam_k1': nrm(ks[15], (L, A_HEAD_DIM), 0.1),
        'lam_q2': nrm(ks[16], (L, A_HEAD_DIM), 0.1),
        'lam_k2': nrm(ks[17], (L, A_HEAD_DIM), 0.1),
        'w_subln': gain(ks[18], (L, A_V_DIM)),
        'conv_w': nrm(ks[19], (L, S_CONV, S_CONV_CH), S_CONV ** -0.5),
        'conv_b': nrm(ks[21], (L, S_CONV_CH), 0.02),
        'dt_bias': dt0 + jnp.log(-jnp.expm1(-dt0)),
        'a_log': jnp.log(jax.random.uniform(ks[22], (L, 2, S_HEADS), f32, 1.0, 16.0)),
        'd_skip': gain(ks[23], (L, S_HEADS)),
        'w_ssd_norm': gain(ks[24], (L, S_INNER)),
        'w_o_attn': nrm(ks[25], (L, A_V_W, D_MODEL), A_V_W ** -0.5),
        'w_o_ssd': nrm(ks[26], (L, S_INNER, D_MODEL), S_INNER ** -0.5),
        'w_out': nrm(ks[27], (L, D_MODEL, D_MODEL), D_MODEL ** -0.5),
        'w_router': nrm(ks[28], (L, D_MODEL, N_EXPERTS), D_MODEL ** -0.5),
        'w_gate': nrm(ks[29], (L, N_EXPERTS, D_MODEL, D_FF), D_MODEL ** -0.5),
        'w_up': nrm(ks[30], (L, N_EXPERTS, D_MODEL, D_FF), D_MODEL ** -0.5),
        'w_down': nrm(ks[31], (L, N_EXPERTS, D_FF, D_MODEL), D_FF ** -0.5),
    }

def reference(x_prompt, x_sample, cache_k, cache_v, state_ssd, c, c_ctx, w_ada, b_ada,
              g_pre_mix, g_post_mix, g_pre_ffn, g_post_ffn, w_in, lam_q1, lam_k1, lam_q2, lam_k2,
              w_subln, conv_w, conv_b, dt_bias, a_log, d_skip, w_ssd_norm, w_o_attn, w_o_ssd,
              w_out, w_router, w_gate, w_up, w_down):
    cond_ctx = jnp.broadcast_to(c_ctx, (x_prompt.shape[0], D_MODEL))
    xp, xs = x_prompt, x_sample
    ks_new, vs_new, sts_new = [], [], []
    for l in range(DEPTH):
        p = dict(w_ada=w_ada[l], b_ada=b_ada[l], g_pre_mix=g_pre_mix[l], g_post_mix=g_post_mix[l],
                 g_pre_ffn=g_pre_ffn[l], g_post_ffn=g_post_ffn[l], w_in=w_in[l],
                 lam_q1=lam_q1[l], lam_k1=lam_k1[l], lam_q2=lam_q2[l], lam_k2=lam_k2[l],
                 w_subln=w_subln[l], conv_w=conv_w[l], conv_b=conv_b[l], dt_bias=dt_bias[l],
                 a_log=a_log[l], d_skip=d_skip[l], w_ssd_norm=w_ssd_norm[l], w_o_attn=w_o_attn[l],
                 w_o_ssd=w_o_ssd[l], w_out=w_out[l], w_router=w_router[l], w_gate=w_gate[l],
                 w_up=w_up[l], w_down=w_down[l])
        xp, (k_new, v_new, st_new) = trunk_layer(xp, cond_ctx, p, l, None)
        ks_new.append(k_new)
        vs_new.append(v_new)
        sts_new.append(st_new)
        xs, _ = trunk_layer(xs, c, p, l, (cache_k[:, l], cache_v[:, l], state_ssd[:, l]))
    new_cache_k = jnp.stack(ks_new, axis=1)
    new_cache_v = jnp.stack(vs_new, axis=1)
    new_state_ssd = jnp.stack(sts_new, axis=1)
    return (xp, xs, new_cache_k, new_cache_v, new_state_ssd)


_drawn_inputs = setup_inputs


def setup_inputs(seed=0):
    import zlib

    import numpy as np

    out = dict(_drawn_inputs(seed))
    spreads = {}
    factors = {'g_post_mix': 3.427, 'g_post_ffn': 8.0, 'lam_q1': 8.0, 'w_subln': 8.0, 'd_skip': 8.0}
    for name, (base, spread) in spreads.items():
        noise = np.random.default_rng([zlib.crc32(name.encode()), seed]).standard_normal(out[name].shape)
        drawn = base * np.exp(spread * noise) if base else spread * noise
        out[name] = jnp.asarray(drawn.astype(out[name].dtype))
    for name, factor in factors.items():
        out[name] = (out[name] * factor).astype(out[name].dtype)
    return out
```

```python
import math
from contextlib import ExitStack

import numpy as np

import concourse.bass as bass
from concourse import mybir

F32 = mybir.dt.float32
U32 = mybir.dt.uint32
ALU = mybir.AluOpType
ACT = mybir.ActivationFunctionType
AX = mybir.AxisListType

P = 128
NT = 3
NTOK = NT * P
D = 1024
KT = D // P
EPS = 1e-6
CW = 512
A_HEADS, A_HD, A_VD = 8, 64, 128
S_INNER, S_HEADS, S_HD, S_GROUPS, S_STATE = 2048, 32, 64, 4, 128
S_HPG = S_HEADS // S_GROUPS
NE, CAP_P, CAP_S, D_FF = 16, 16, 32, 2048
CAP = CAP_P + CAP_S
LAM_INIT = 0.8 - 0.6 * math.exp(-0.3 * 0)
Q0, K0, V0 = 0, 1024, 2048
Z0, X0, B0, C0 = 3072, 5120, 7168, 7680
DT0, GA0, GS0 = 8192, 8256, 9280
PAD = NTOK + 1
TOK = (0, P + 1, 2 * P + 1)
FF_SLOTS = 6

C_ID, C_TF, C_TB, C_PM, C_ON, C_COS, C_SIN, C_IO, C_END = 0, 128, 256, 384, 512, 640, 896, 1152, 1154


def shape_constants():
    c = np.zeros((P, C_END), np.float32)
    i = np.arange(P)
    c[:, C_ID:C_ID + P] = np.eye(P)
    c[:, C_TF:C_TF + P] = i[:, None] <= i[None, :]
    c[:, C_TB:C_TB + P] = i[:, None] >= i[None, :]
    half, nf = A_HD // 2, A_HD // 4
    for d in range(P):
        if d % half < nf:
            c[d + nf, C_PM + d] = -1.0
        else:
            c[d - nf, C_PM + d] = 1.0
    c[:, C_ON:C_ON + P] = 1.0
    tok = np.arange(2 * P)
    pos = np.stack([tok // 64, tok % 64]).astype(np.float32)
    inv = np.power(np.float32(10000.0), -np.arange(nf, dtype=np.float32) / np.float32(nf)).astype(np.float32)
    axis = (i % A_HD) // half
    ang = pos[axis] * inv[i % nf][:, None]
    c[:, C_COS:C_COS + 2 * P] = np.cos(ang.astype(np.float32))
    c[:, C_SIN:C_SIN + 2 * P] = np.sin(ang.astype(np.float32))
    c[:, C_IO] = i
    c[:, C_IO + 1] = i + P
    return c


class Count:

    def __init__(self, eng, sem):
        self.eng, self.sem, self.n = eng, sem, 0

    def do(self, ins):
        self.n += 1
        return ins.then_inc(self.sem, 1)

    def settle(self):
        self.eng.wait_ge(self.sem, self.n)


def build(nc, t_in, t_out, consts, scratch):
    ctx = ExitStack()
    with ctx:
        arena = ctx.enter_context(nc.sbuf_tensor("arena", [P, 53184], F32))
        psum = ctx.enter_context(nc.psum_tensor("psum", [P, 8, 512], F32))
        sems = {}

        def sem(name):
            if name not in sems:
                sems[name] = ctx.enter_context(nc.semaphore(name))
            return sems[name]

        def at(kib, *shape):
            n = int(np.prod(shape))
            off = int(kib * 256)
            assert off + n <= 53184, (kib, shape)
            v = arena[:, off:off + n]
            if len(shape) == 1:
                return v
            names = "abcd"[:len(shape)]
            return v.rearrange(f"p ({' '.join(names)}) -> p {' '.join(names)}",
                               **{k: s for k, s in zip(names[1:], shape[1:])})

        slots = [at(16 * s, KT, CW) for s in range(FF_SLOTS)]
        cst = at(96, C_END)
        ident, tri_f, tri_b = cst[:, C_ID:C_ID + P], cst[:, C_TF:C_TF + P], cst[:, C_TB:C_TB + P]
        perm, ones = cst[:, C_PM:C_PM + P], cst[:, C_ON:C_ON + P]
        cos_t, sin_t = cst[:, C_COS:C_COS + 2 * P], cst[:, C_SIN:C_SIN + 2 * P]
        iota = cst[:, C_IO:C_IO + 2]
        sm = [101.0]

        def small(*shape):
            v = at(sm[0], *shape)
            sm[0] += int(np.prod(shape)) / 256
            assert sm[0] <= 110
            return v

        vec_a = small(96)
        vec_b = small(113)
        cond = small(KT, 2)
        mod = small(48, 2)
        aff1 = small(2 * KT, 2)
        aff2 = small(2 * KT, 2)
        gpost = small(2 * KT, 2)
        dt_w = at(203.5, KT, 64)
        dt_bias, a_neg = small(64), small(64)
        d_skip = small(S_HEADS)
        dt, cs, e_cs, dec_dt = small(NT, 64), small(NT, 64), small(NT, 64), small(NT, 64)
        e_tot, t_tot, tmp_a = small(NT, 64), small(NT, 64), small(NT, 64)
        lam_in, lam_t = small(4, A_HD), small(8)
        stat = small(48)
        neg_max, row_max, row_sum, inv_sum = small(2, 2), small(2, 2), small(2, 2), small(2, 2)
        route = small(8)
        h1T = at(110, KT, NTOK)
        mergedT = at(122, KT, NTOK)
        x0 = at(32, NT, D)
        rows_a, rows_b = at(44, P), at(44.5, P)
        junk0, junk1 = at(46, D), at(50, D)
        raw2 = at(32, 2, PAD + 2)
        conv2 = at(35.25, 2, PAD)
        th = at(38.5, 512)
        xs = at(40.5, 4, PAD)
        xTM = at(46.75, NT, 512)
        zs2 = at(52.75, 2, NT, 512)
        h0raw = at(64.75, 2, 4, P)
        h0T = at(68.75, 2, 512)
        hT1 = at(72.75, 2, 512)
        xdec = at(76.75, 2, 512)
        y1 = at(80.75, 2, 512)
        ytmp = at(84.75, 512)
        junk = at(86.75, 512)
        cbm = at(88.75, 2, 2, P)
        st_out = at(90.75, 2, 512)
        BC = at(134, 8, PAD)
        BTM = at(146.25, NT, 512)
        oT = at(152.25, 16, NTOK)
        csT = at(152.25, 2, NT, P)
        ebuf = at(176.25, 4, S_HPG, P)
        gsT = at(192.25, KT, NTOK)
        qT = at(134, A_HEADS, NTOK)
        kT = at(146, A_HEADS, 512)
        vT = at(162, 4, D)
        oTa = at(178, A_HEADS, NTOK)
        gaT = at(190, KT, NTOK)
        k_out = at(202, D)
        rope_raw = at(64, 2, 2 * P)
        rope_tmp = at(66, 2 * P)
        ck_raw = at(67, D)
        prob = at(71, 2, 2, NTOK)
        amix = at(77, 2, NTOK)
        aT = at(80, 2, NTOK)
        o_sb = at(83, 4, P)
        o_junk = at(85, P)
        proj_tmp = at(86, 2, NTOK)
        x = at(110, NT, D)
        hT = at(122, 16, CAP)
        xe = at(125, KT, CAP)
        sg = at(126.5, 2, 4 * CAP)
        wr = at(128, KT, NE)
        lg, affin = at(128.5, NT, NE), at(128.75, NT, NE)
        affT, work = at(129, NTOK), at(130.5, NTOK)
        idx_u, idx_f = at(132, CAP).bitcast(U32), at(132.25, CAP)
        mx8 = at(132.5, CAP)
        y = at(134, NT, D)
        S_p, S_s = at(134, NE * CAP_P), at(135, 2, NE * CAP_S)
        SG_p, SG_s = at(139, NE * CAP_P), at(140, 2, NE * CAP_S)
        idx_blk = at(144, NE * CAP_S)
        xn = at(146, NT, D)
        h2T = at(158, KT, NTOK)
        yT_s, yT_p = at(146, KT, NE, CAP_S), at(162, KT, NE, CAP_P)
        xeT = at(170, KT, NE, CAP)
        Gt = at(194, 5, 2 * P)
        Gb = at(199, 2, D)
        ye = at(0, 6, D)
        diag = at(92, 4, P)
        last_junk = at(32, D)

        w_in, w_ada = t_in["w_in"][0], t_in["w_ada"][0]

        def cols(w, c, k=0):
            return w[k * D:(k + 1) * D, c:c + CW].rearrange("(k p) n -> p k n", p=P)

        chunks = []

        def add(w, c, k=0):
            chunks.append(cols(w, c, k))

        for j in range(4):
            add(w_ada, j * CW)
        add(w_in, B0)
        add(w_in, C0)
        for g in range(S_GROUPS):
            add(w_in, X0 + g * CW)
            add(w_in, Z0 + g * CW)
        for j in range(2):
            add(w_in, GS0 + j * CW)
        for j in range(2):
            for k in range(2):
                add(t_in["w_o_ssd"][0], j * CW, k)
        for j in range(4, 12):
            add(w_ada, j * CW)
        for c in (Q0, K0, V0, GA0):
            for j in range(2):
                add(w_in, c + j * CW)
        for w in ("w_o_attn", "w_out"):
            for j in range(2):
                add(t_in[w][0], j * CW)
        NM = len(chunks)
        assert NM % 2 == 0
        AT = {}

        units = [(g, t) for g in range(S_GROUPS) for t in range(NT)]

        def beside(g, t):
            if g + 1 < S_GROUPS:
                return [[("x", g + 1, 0), ("x", g + 1, 1)], [("x", g + 1, 2), ("x", g + 1, 3)],
                        [("z", g + 1, 0), ("z", g + 1, 1), ("z", g + 1, 2)]][t]
            return [[("g", i) for i in range(3)], [("g", i) for i in range(3, 6)], [("g", 6), ("g", 7)]][t]

        block = ctx.enter_context(nc.Block())

        @block.tensor
        def _(pe):
            n_p, n_x, n_w, n_t = [0], [0], [0], [0]
            AT["chunk_end"] = []

            def p_written():
                pe.wait_ge(sem("p_free"), n_p[0])

            def x_written():
                pe.wait_ge(sem("x_free"), n_x[0])

            def p_bank(k=1):
                n = n_p[0]
                n_p[0] += k
                if n + k > 4:
                    pe.wait_ge(sem("p_free"), n + k - 4)
                return psum[:, n % 4] if k == 1 else None

            def p_done(mm):
                mm.then_inc(sem("p_ready"), 1)

            def x_bank():
                n = n_x[0]
                n_x[0] += 1
                if n >= 4:
                    pe.wait_ge(sem("x_free"), n - 3)
                return psum[:, 4 + n % 4]

            def x_done(mm):
                mm.then_inc(sem("x_ready"), 1)

            def chunk():
                n = n_w[0]
                n_w[0] += 1
                pe.wait_ge(sem(f"w_in_slot{n % 2}"), 16 * (n // 2 + 1))
                return slots[n % 2]

            def chunk_used():
                AT["chunk_end"].append(("p_ready", n_p[0]))

            def cm_tile(w, ct, src=None, last=False):
                src = h1T if src is None else src
                b = p_bank()
                for k in range(KT):
                    mm = pe.matmul(b[:, 0:NTOK], w[:, k, ct * P:(ct + 1) * P], src[:, k, :],
                                   start=k == 0, stop=k == KT - 1)
                p_done(mm)
                if last:
                    chunk_used()

            def tm_tile(w, t, src=None, last=False):
                src = h1T if src is None else src
                b = p_bank()
                for k in range(KT):
                    mm = pe.matmul(b[:, :], src[:, k, t * P:(t + 1) * P], w[:, k, :],
                                   start=k == 0, stop=k == KT - 1)
                p_done(mm)
                if last:
                    chunk_used()

            def ada():
                w = chunk()
                b = p_bank()
                for ct in range(4):
                    for k in range(KT):
                        mm = pe.matmul(b[:, 2 * ct:2 * ct + 2], w[:, k, ct * P:(ct + 1) * P], cond[:, k, :],
                                       start=k == 0, stop=k == KT - 1)
                p_done(mm)
                chunk_used()

            def transposes(pairs):
                b = x_bank()
                at_ = 0
                for src in pairs:
                    rows, width = src.shape[0], int(np.prod(src.shape[1:]))
                    mm = pe.transpose(b[0:width, at_:at_ + rows], src, ident[0:rows, 0:rows])
                    at_ += rows
                x_done(mm)

            pe.wait_ge(sem("const_in"), 16)
            pe.wait_ge(sem("rows_a_in"), 16 * 7)
            transposes([rows_a[0:96, :]])
            pe.wait_ge(sem("rows_b_in"), 16 * 4)
            transposes([rows_b[0:113, :]])
            pe.wait_ge(sem("cond_ready"), 1)
            for _ in range(4):
                ada()
            pe.wait_ge(sem("xn_ready"), NT)
            for k in range(KT):
                transposes([x0[:, t, k * P:(k + 1) * P] for t in range(NT)])
            x_written()
            for _ in range(2):
                w = chunk()
                for ct in range(4):
                    cm_tile(w, ct, last=ct == 3)
            n_t[0] += 8
            after_bc = n_t[0]
            pe.wait_ge(sem("dtw_in"), 16)
            for ts in ((0,), (1, 2)):
                b = p_bank()
                for i, t in enumerate(ts):
                    for k in range(KT):
                        mm = pe.matmul(b[:, i * 64:(i + 1) * 64], h1T[:, k, t * P:(t + 1) * P], dt_w[:, k, :],
                                       start=k == 0, stop=k == KT - 1)
                p_done(mm)
            AT["dt"] = n_p[0]
            w = chunk()
            for ct in range(4):
                cm_tile(w, ct, last=ct == 3)
            w = chunk()
            for t in range(NT):
                tm_tile(w, t, last=t == 2)
            x_items = {0: n_t[0] + 4}
            n_t[0] += 7
            pe.wait_ge(sem("t_used"), after_bc)
            for t in range(NT):
                transposes([BC[:, g, TOK[t]:TOK[t] + P] for g in range(4)])
            btm_at = n_x[0]
            pe.wait_ge(sem("da_ready"), 1)
            b = x_bank()
            for t in range(NT):
                pe.matmul(b[:, t * 64:t * 64 + 32], tri_f, tmp_a[:, t, 0:32], start=True, stop=True)
                mm = pe.matmul(b[:, t * 64 + 32:t * 64 + 64], tri_b, tmp_a[:, t, 32:64], start=True, stop=True)
            x_done(mm)
            b = x_bank()
            mm = pe.matmul(b[:, 0:NT * 64], ones, tmp_a[:, :, :], start=True, stop=True)
            x_done(mm)
            for d, tri in ((0, tri_f), (1, tri_b)):
                b = x_bank()
                for t in range(NT):
                    mm = pe.matmul(b[0:32, t * P:(t + 1) * P], tmp_a[:, t, 32 * d:32 * d + 32], tri,
                                   start=True, stop=True)
                x_done(mm)

            AT["csT"] = n_x[0]

            w = None

            def side(item):
                nonlocal w
                if item[0] != "g":
                    n_t[0] += 1
                if item[0] == "x":
                    x_items[item[1]] = n_t[0]
                if item[0] == "x":
                    if item[2] == 0:
                        w = chunk()
                    cm_tile(w, item[2], last=item[2] == 3)
                elif item[0] == "z":
                    if item[2] == 0:
                        w = chunk()
                    tm_tile(w, item[2], last=item[2] == 2)
                else:
                    if item[1] % 4 == 0:
                        w = chunk()
                    cm_tile(w, item[1] % 4, last=item[1] % 4 == 3)

            def back_to_cm(u):
                pe.wait_ge(sem("yn_ready"), u + 1)
                transposes([y1[:, u % 2, c * P:(c + 1) * P] for c in range(4)])

            for u, (g, t) in enumerate(units):
                if t == 0:
                    pe.wait_ge(sem("t_used"), x_items[g])
                    for tt in range(NT):
                        transposes([xs[:, c, TOK[tt]:TOK[tt] + P] for c in range(4)])
                    for d in range(2):
                        pe.wait_ge(sem(f"h0_in_d{d}"), 16 * (g + 1))
                        transposes([h0raw[:, d, c, :] for c in range(4)])
                    AT.setdefault("h0", []).append(n_x[0])
                b = x_bank()
                mm = pe.matmul(b[:, 0:P], BC[:, g, TOK[t]:TOK[t] + P], BC[:, 4 + g, TOK[t]:TOK[t] + P],
                               start=True, stop=True)
                x_done(mm)
                if t == 0:
                    for d in range(2):
                        pe.wait_ge(sem("xdec_ready"), 4 * g + d + 1)
                        pe.wait_ge(sem("x_free"), btm_at)
                        b = x_bank()
                        for c in range(4):
                            mm = pe.matmul(b[:, c * P:(c + 1) * P], xdec[:, d, c * P:(c + 1) * P],
                                           BTM[:, 0, g * P:(g + 1) * P], start=True, stop=True)
                        x_done(mm)
                        AT.setdefault("st", []).append(n_x[0])
                if t == 1:
                    for d in range(2):
                        pe.wait_ge(sem("xdec_ready"), 4 * g + 2 + d + 1)
                        b = x_bank()
                        mm = pe.matmul(b[:, :], BTM[:, 1 + d, g * P:(g + 1) * P], xdec[:, d, :],
                                       start=True, stop=True)
                        x_done(mm)
                    hT1_at = n_x[0]
                for item in beside(g, t):
                    side(item)
                if u:
                    back_to_cm(u - 1)
                pe.wait_ge(sem("m_ready"), 2 * u + 2)
                b = x_bank()
                AT.setdefault("y", []).append(n_x[0])
                for h in range(S_HPG):
                    o = b[:, h * S_HD:(h + 1) * S_HD]
                    xh = xTM[:, t, h * S_HD:(h + 1) * S_HD]
                    pe.matmul(o, ebuf[:, (2 * u) % 4, h, :], xh, start=True, stop=False)
                    mm = pe.matmul(o, ebuf[:, (2 * u + 1) % 4, h, :], xh, start=False, stop=True)
                x_done(mm)
                if t:
                    if t == 1:
                        pe.wait_ge(sem("x_free"), hT1_at)
                    for d in range(2):
                        fresh = (t == 1) == (d == 0)
                        b = x_bank()
                        mm = pe.matmul(b[:, :], BC[:, 4 + g, TOK[t]:TOK[t] + P],
                                       h0T[:, d, :] if fresh else hT1[:, d, :], start=True, stop=True)
                        x_done(mm)
            back_to_cm(len(units) - 1)

            AT["gs"] = n_p[0]
            x_written()
            for j in range(2):
                n0 = n_p[0]
                p_bank(4)
                for k2 in range(2):
                    w = chunk()
                    for ct in range(4):
                        for k in range(KT):
                            mm = pe.matmul(psum[:, (n0 + ct) % 4, 0:NTOK], w[:, k, ct * P:(ct + 1) * P],
                                           oT[:, k2 * KT + k, :], start=k2 == 0 and k == 0,
                                           stop=k2 == 1 and k == KT - 1)
                        if k2 == 1:
                            p_done(mm)
                    if k2 == 1:
                        chunk_used()
                    else:
                        mm.then_inc(sem("half_used"), 1)
                        AT["chunk_end"].append(("half_used", j + 1))
            for _ in range(8):
                ada()
            AT["ada"] = n_p[0]

            def rope(i):
                pe.wait_ge(sem("p_free"), AT["q"] + i + 1)
                b = x_bank()
                x_done(pe.matmul(b[:, 0:2 * P], perm, rope_raw[:, i % 2, :], start=True, stop=True))

            AT["q"] = n_p[0]
            for i in range(2 * A_HEADS):
                if i % 4 == 0:
                    w = chunk()
                cm_tile(w, i % 4, last=i % 4 == 3)
                if i:
                    rope(i - 1)
            rope(2 * A_HEADS - 1)
            pe.wait_ge(sem("ck_in"), 16)
            for j in range(2):
                transposes([ck_raw[:, (4 * j + c) * P:(4 * j + c + 1) * P] for c in range(4)])
            AT["ck"] = n_x[0]
            p_written()
            for j in range(2):
                transposes([kT[:, 4 * j + c, 0:P] for c in range(4)])
                AT.setdefault("kout", []).append(n_x[0])
            for _ in range(2):
                w = chunk()
                for t in range(NT):
                    tm_tile(w, t, last=t == 2)
            AT["v"] = n_p[0]
            for _ in range(2):
                w = chunk()
                for ct in range(4):
                    cm_tile(w, ct, last=ct == 3)

            pairs = [(h, t) for h in range(A_HEADS) for t in range(NT)]
            NA = len(pairs)
            assert n_p[0] % 2 == 0
            AT["attn"] = n_p[0]
            pe.wait_ge(sem("rope_done"), 2 * A_HEADS)
            pe.wait_ge(sem("x_free"), AT["ck"])
            pe.wait_ge(sem("p_free"), AT["v"])
            aT_at = []
            pe.wait_ge(sem("cv_in"), 16)

            def key_blocks(t):
                return [(0, 0)] if t == 0 else [(b_, b_ + 1) for b_ in range(3)]

            for i in range(NA + 3):
                if i < NA:
                    h, t = pairs[i]
                    k0, kn = (0, P) if t == 0 else (P, NTOK)
                    n = n_p[0]
                    p_bank(2)
                    for m in range(2):
                        r = slice(m * A_HD, (m + 1) * A_HD)
                        mm = pe.matmul(psum[:, (n + m) % 4, 0:kn], qT[r, h, t * P:(t + 1) * P],
                                       kT[r, h, k0:k0 + kn], start=True, stop=True)
                        p_done(mm)
                if 1 <= i <= NA:
                    h, t = pairs[i - 1]
                    pe.wait_ge(sem("a_ready"), i)
                    transposes([amix[:, (i - 1) % 2, c * P:(c + 1) * P] for c, _ in key_blocks(t)])
                    aT_at.append(n_x[0])
                if 2 <= i <= NA + 1:
                    h, t = pairs[i - 2]
                    pe.wait_ge(sem("x_free"), aT_at[i - 2])
                    b = x_bank()
                    kb = key_blocks(t)
                    for c, vb in kb:
                        mm = pe.matmul(b[:, 0:P], aT[:, (i - 2) % 2, c * P:(c + 1) * P],
                                       vT[:, vb, h * P:(h + 1) * P], start=c == 0, stop=c == len(kb) - 1)
                    x_done(mm)
                if i >= 3:
                    pe.wait_ge(sem("on_ready"), i - 2)
                    transposes([o_sb[:, (i - 3) % 4, :]])

            AT["oTa"] = n_x[0]
            x_written()
            for _ in range(2):
                w = chunk()
                for ct in range(4):
                    cm_tile(w, ct, src=oTa, last=ct == 3)
            pe.wait_ge(sem("merged_ready"), 2 * KT)

            def spread():
                for c in range(2):
                    for j in range(2):
                        b = x_bank()
                        for q in range(4):
                            spread.n += 1
                            pe.wait_ge(sem("diag_ready"), spread.n)
                            mm = pe.matmul(b[:, q * P:(q + 1) * P], ones, diag[:, q, :], start=True, stop=True)
                        x_done(mm)
            spread.n = 0
            for _ in range(2):
                w = chunk()
                for t in range(NT):
                    tm_tile(w, t, src=mergedT, last=t == 2)
            spread()

            pe.wait_ge(sem("xn2_ready"), NT)
            for k in range(KT):
                transposes([xn[:, t, k * P:(k + 1) * P] for t in range(NT)])
            x_written()
            pe.wait_ge(sem("wr_in"), 16)
            b = x_bank()
            for t in range(NT):
                for k in range(KT):
                    mm = pe.matmul(b[:, t * NE:(t + 1) * NE], h2T[:, k, t * P:(t + 1) * P], wr[:, k, :],
                                   start=k == 0, stop=k == KT - 1)
            x_done(mm)
            pe.wait_ge(sem("affin_ready"), 1)
            transposes([affin[:, t, :] for t in range(NT)])
            for i, n in ((0, NE * CAP_P), (1, NE * CAP_S)):
                pe.wait_ge(sem("idx_ready"), i + 1)
                b = x_bank()
                x_done(pe.matmul(b[:, 0:n], ones[0:NE, :], idx_blk[0:NE, 0:n], start=True, stop=True))
            x_written()
            for k in range(KT):
                b = x_bank()
                x_done(pe.matmul(b[:, 0:NE * CAP_P], xn[:, 0, k * P:(k + 1) * P], S_p, start=True, stop=True))
                b = x_bank()
                pe.matmul(b[:, :], xn[:, 1, k * P:(k + 1) * P], S_s[:, 0, :], start=True, stop=False)
                x_done(pe.matmul(b[:, :], xn[:, 2, k * P:(k + 1) * P], S_s[:, 1, :], start=False, stop=True))
            pe.wait_ge(sem("SG_ready"), NT)
            for j in range(4):
                transposes([SG_s[:, t, j * P:(j + 1) * P] for t in range(2)])
            transposes([SG_p[:, j * P:(j + 1) * P] for j in range(2)])
            AT["ffn_x"] = n_x[0]

            pe.wait_ge(sem("x_free"), n_x[0])
            pe.wait_ge(sem("p_free"), n_p[0])
            with pe.Fori(0, NE) as e:
                pe.wait_ge(sem("xe_ready"), e + 1)
                for c in range(12):
                    s = (c + 2) % FF_SLOTS
                    pe.wait_ge(sem(f"ff_slot{s}"), e * 32 + 16 * (c // 6 + 1))
                    w = slots[s]
                    if c < 8:
                        j, up = c // 2, c % 2
                        bank = psum[:, 2 * up + j % 2]
                        if not up:
                            pe.wait_ge(sem(f"h_done{j % 2}"), e * 2 + (j // 2 + 1))
                        for ct in range(4):
                            for k in range(KT):
                                mm = pe.matmul(bank[:, ct * CAP:(ct + 1) * CAP], w[:, k, ct * P:(ct + 1) * P],
                                               xe[:, k, :], start=k == 0, stop=k == KT - 1)
                        mm.then_inc(sem("gu_ready" if up else "ff_used"), 1)
                    else:
                        j, k2 = (c - 8) // 2, c % 2
                        bank = psum[:, 4 + j]
                        if c == 8:
                            pe.wait_ge(sem("h_done0"), e * 2 + 3)
                            pe.wait_ge(sem("h_done1"), e * 2 + 3)
                        if not k2:
                            pe.wait_ge(sem(f"d_free{j}"), e + 1)
                        for ct in range(4):
                            for k in range(KT):
                                mm = pe.matmul(bank[:, ct * CAP:(ct + 1) * CAP], w[:, k, ct * P:(ct + 1) * P],
                                               hT[:, k2 * KT + k, :], start=k2 == 0 and ct == 0 and k == 0,
                                               stop=k2 == 1 and k == KT - 1, skip_group_check=True)
                        mm.then_inc(sem(f"d_ready{j}" if k2 else "ff_used"), 1)

            pe.wait_ge(sem("d_free0"), NE + 1)
            pe.wait_ge(sem("d_free1"), NE + 1)
            for j in range(6):
                for kk in range(2):
                    sl = yT_s[:, :, 4 * j:4 * j + 4] if j < 4 else yT_p[:, :, 8 * (j - 4):8 * (j - 4) + 8]
                    transposes([sl[:, 4 * kk + q].rearrange("p e c -> p (e c)") for q in range(4)])
            x_written()
            spread()
            for t in range(NT):
                for half in range(2):
                    b = p_bank()
                    js = (4, 5) if t == 0 else (0, 1, 2, 3)
                    for j in js:
                        lt = Gt[:, 4, (j - 4) * P:(j - 3) * P] if t == 0 else Gt[:, j, (t - 1) * P:t * P]
                        mm = pe.matmul(b[:, :], lt, ye[:, j, half * 512:(half + 1) * 512],
                                       start=j == js[0], stop=j == js[-1])
                    p_done(mm)

        @block.sync
        def _(sp):
            sp.dma_start(cst, consts).then_inc(sem("const_in"), 16)
            for n, src in enumerate(chunks):
                if n >= 2:
                    name, value = AT["chunk_end"][n - 2]
                    sp.wait_ge(sem(name), value)
                sp.dma_start(slots[n % 2], src).then_inc(sem(f"w_in_slot{n % 2}"), 16)
            wg, wu, wd = t_in["w_gate"][0], t_in["w_up"][0], t_in["w_down"][0]

            def expert_chunk(e, c):
                w, c0, k0 = ((wg, wu)[c % 2], c // 2, 0) if c < 8 else (wd, (c - 8) // 2, c % 2)
                return w[e, k0 * D:(k0 + 1) * D, c0 * CW:(c0 + 1) * CW].rearrange("(k p) n -> p k n", p=P)

            def load(e, c):
                s = (c + 2) % FF_SLOTS
                sp.dma_start(slots[s], expert_chunk(e, c)).then_inc(sem(f"ff_slot{s}"), 16)

            def wait_used(e, c):
                if c >= 8 and c % 2:
                    sp.wait_ge(sem(f"d_ready{(c - 8) // 2}"), e + 1)
                elif c % 2:
                    sp.wait_ge(sem("gu_ready"), e * 4 + (c // 2 + 1))
                else:
                    sp.wait_ge(sem("ff_used"), e * 6 + (c // 2 + 1))

            for c in range(12):
                if c == 0:
                    sp.wait_ge(sem("ssd_over"), 1)
                if c == 2:
                    sp.wait_ge(sem("attn_over"), 1)
                if c == 4:
                    sp.wait_ge(sem("p_ready"), AT["chunk_end"][NM - 1][1])
                if c >= 6:
                    wait_used(0, c - 6)
                load(0, c)
            with sp.Fori(1, NE) as e:
                for c in range(12):
                    wait_used(e - 1 if c < 6 else e, (c - 6) % 12)
                    load(e, c)

        n_store = [0]

        @block.gpsimd
        def _(pool):
            def rows(dst, at_, src, n, s):
                pool.dma_start(dst[at_:at_ + n, :], src.rearrange("(a p) -> a p", p=P)).then_inc(sem(s), 16)

            rows(rows_a, 0, t_in["b_ada"][0], 48, "rows_a_in")
            for i, name in enumerate(("g_pre_mix", "g_post_mix", "g_pre_ffn", "g_post_ffn")):
                rows(rows_a, 48 + 8 * i, t_in[name][0], 8, "rows_a_in")
            rows(rows_a, 80, t_in["c_ctx"], 8, "rows_a_in")
            rows(rows_a, 88, t_in["c"][0], 8, "rows_a_in")
            pool.dma_start(x0[:, 0, :], t_in["x_prompt"][0]).then_inc(sem("x_in"), 16)
            pool.dma_start(x0[:, 1:3, :], t_in["x_sample"][0].rearrange("(t p) d -> p t d", p=P)).then_inc(sem("x_in"), 16)
            rows(rows_b, 0, t_in["conv_w"][0].rearrange("k c -> (k c)"), 72, "rows_b_in")
            rows(rows_b, 72, t_in["conv_b"][0], 24, "rows_b_in")
            rows(rows_b, 96, t_in["w_ssd_norm"][0], 16, "rows_b_in")
            rows(rows_b, 112, t_in["w_subln"][0], 1, "rows_b_in")
            pool.dma_start(dt_bias, t_in["dt_bias"][0].rearrange("a h -> (a h)").partition_broadcast(P)).then_inc(sem("dtp_in"), 16)
            pool.dma_start(a_neg, t_in["a_log"][0].rearrange("a h -> (a h)").partition_broadcast(P)).then_inc(sem("dtp_in"), 16)
            pool.dma_start(d_skip, t_in["d_skip"][0].partition_broadcast(P)).then_inc(sem("dtp_in"), 16)
            for i, name in enumerate(("lam_q1", "lam_k1", "lam_q2", "lam_k2")):
                pool.dma_start(lam_in[:, i, :], t_in[name][0].partition_broadcast(P)).then_inc(sem("lam_in"), 16)
            pool.dma_start(dt_w, w_in[:, DT0:DT0 + 64].rearrange("(k p) n -> p k n", p=P)).then_inc(sem("dtw_in"), 16)
            pool.memset(stat[:, 40:41], -0.5).then_inc(sem("pool_const"), 1)
            pool.wait_ge(sem("pool_const"), 1)

            def power(out, src, waits):
                pool.wait_ge(sem(waits[0]), waits[1])
                pool.tensor_tensor(out, src, stat[:, 40:41], ALU.pow).then_inc(sem("pow_done"), 1)

            def store(dst, src, waits):
                pool.wait_ge(sem(waits[0]), waits[1])
                n_store[0] += 1
                pool.dma_start(dst, src).then_inc(sem("stored"), 16)

            for t in range(NT):
                power(stat[:, t:t + 1], stat[:, 4 + t:5 + t], ("ms_ready", t + 1))
            pool.wait_ge(sem("x_free"), AT["csT"])
            pool.dma_start(scratch.rearrange("d t h l -> h d t l"), csT[0:32]).then_inc(sem("csT_out"), 16)
            pool.wait_ge(sem("csT_out"), 16)

            def load_cs(n):
                g, t = units[n // 2]
                if n >= 4:
                    pool.wait_ge(sem("x_ready"), AT["y"][n // 2 - 2])
                pool.dma_start(ebuf[:, n % 4].rearrange("p h l -> p (h l)"),
                               scratch[n % 2, t, S_HPG * g:S_HPG * (g + 1), :].rearrange("h l -> (h l)")
                               .partition_broadcast(P)).then_inc(sem(f"cs_in{n % 4}"), 16)

            state = t_in["state_ssd"][0, 0]
            new_state = t_out["state"][0, 0]

            def load_h0(g):
                if g:
                    pool.wait_ge(sem("x_ready"), AT["h0"][g - 1])
                for d in range(2):
                    pool.dma_start(h0raw[:, d], state[d, S_HPG * g:S_HPG * (g + 1)].rearrange(
                        "(c a) p n -> (a p) c n", a=2)).then_inc(sem(f"h0_in_d{d}"), 16)

            load_h0(0)
            for n in range(4):
                load_cs(n)
            for u, (g, t) in enumerate(units):
                if t == 0:
                    if g + 1 < S_GROUPS:
                        load_h0(g + 1)
                    for d in range(2):
                        store(new_state[d, S_HPG * g:S_HPG * (g + 1)].rearrange("(c a) p n -> (a p) c n", a=2),
                              st_out[:, d].rearrange("p (c n) -> p c n", n=P), ("x_free", AT["st"][2 * g + d]))
                power(stat[:, 8 + u % 2:9 + u % 2], stat[:, 10 + u % 2:11 + u % 2], ("yms_ready", u + 1))
                if u + 2 < len(units):
                    load_cs(2 * u + 4)
                    load_cs(2 * u + 5)
            pool.wait_ge(sem("ssd_over"), 1)
            pool.dma_start(ck_raw, t_in["cache_k"][0, 0].rearrange("s h d -> s (h d)")).then_inc(sem("ck_in"), 16)
            pool.wait_ge(sem("p_ready"), AT["q"] + 1)
            pool.dma_start(vT[:, 1, :], t_in["cache_v"][0, 0].rearrange("s h d -> s (h d)")).then_inc(sem("cv_in"), 16)
            store(t_out["k"][0, 0].rearrange("s h d -> s (h d)"), k_out, ("x_free", AT["kout"][1]))
            store(t_out["v"][0, 0].rearrange("s h d -> s (h d)"), vT[:, 0, :], ("p_free", AT["v"]))
            for i in range(A_HEADS * NT):
                power(stat[:, 12 + i % 4:13 + i % 4], stat[:, 16 + i % 4:17 + i % 4], ("oms_ready", i + 1))
            pool.wait_ge(sem("p_ready"), AT["attn"])
            pool.dma_start(x[:, 0, :], t_in["x_prompt"][0]).then_inc(sem("x_again"), 16)
            pool.dma_start(x[:, 1:3, :], t_in["x_sample"][0].rearrange("(t p) d -> p t d", p=P)).then_inc(sem("x_again"), 16)
            for t in range(NT):
                power(stat[:, 20 + t:21 + t], stat[:, 24 + t:25 + t], ("ms2_ready", t + 1))
            pool.dma_start(wr, t_in["w_router"][0].rearrange("(k p) n -> p k n", p=P)).then_inc(sem("wr_in"), 16)
            for t in range(NT):
                power(stat[:, t:t + 1], stat[:, 4 + t:5 + t], ("ms3_ready", t + 1))
            for t in range(NT):
                power(stat[:, 20 + t:21 + t], stat[:, 24 + t:25 + t], ("ms4_ready", t + 1))
            store(t_out["xp"][0], x[:, 0, :], ("out_ready", 1))
            for t in (1, 2):
                store(t_out["xs"][0, (t - 1) * P:t * P, :], x[:, t, :], ("out_ready", t + 1))
            pool.wait_ge(sem("stored"), 16 * n_store[0])

        @block.scalar
        def _(act):
            n_p, n_t, n_c = [0], [0], [0]
            use_of_conv = []

            def p_take():
                n = n_p[0]
                n_p[0] += 1
                act.wait_ge(sem("p_ready"), n + 1)
                return psum[:, n % 4]

            def p_free(ins):
                return ins.then_inc(sem("p_free"), 1)

            def t_write():
                if n_t[0]:
                    act.wait_ge(sem("t_used"), n_t[0])
                n_t[0] += 1

            act.wait_ge(sem("x_free"), 1)
            act.activation(junk1[:, 0:16], vec_a[:, 80:96], ACT.Tanh, scale=0.5).then_inc(sem("cond_t"), 1)
            act.wait_ge(sem("x_in"), 32)
            for t in range(NT):
                if t:
                    act.wait_ge(sem("sq_ready"), t)
                act.activation(junk0, x0[:, t, :], ACT.Square, accum_out=stat[:, 32 + t:33 + t]).then_inc(sem("sq_ready"), 1)

            def ada(j):
                b = p_take()
                p_free(act.activation(mod[:, 4 * j:4 * j + 4, :].rearrange("p a b -> p (a b)"), b[:, 0:8], ACT.Copy))

            for j in range(4):
                ada(j)

            def conv_in(i, ch):
                b = p_take()
                r, cc = raw2[:, i % 2], conv2[:, i % 2]
                if i >= 2:
                    act.wait_ge(sem("t_used"), use_of_conv[i - 2])
                act.activation(r[:, 1:P + 1], b[:, 0:P], ACT.Copy)
                p_free(act.activation(r[:, P + 2:PAD + 1], b[:, P:NTOK], ACT.Copy))
                act.wait_ge(sem("p_free"), n_p[0])
                act.activation(cc, r[:, 1:PAD + 1], ACT.Identity, scale=vec_b[:, 24 + ch:25 + ch],
                               bias=vec_b[:, 72 + ch:73 + ch]).then_inc(sem("conv_in"), 1)

            def conv_tanh(i):
                act.wait_ge(sem("conv_mid"), i + 1)
                t_write()
                use_of_conv.append(n_t[0])
                act.activation(th[:, 0:PAD], conv2[:, i % 2], ACT.Tanh).then_inc(sem("t_ready"), 1)

            def z_in(g, t):
                b = p_take()
                p_free(act.activation(zs2[:, g % 2, t, :], b[:, :], ACT.Copy, scale=0.5))
                return n_p[0]

            def z_tanh(g, t, n):
                act.wait_ge(sem("p_free"), n)
                t_write()
                act.activation(th, zs2[:, g % 2, t, :], ACT.Tanh).then_inc(sem("t_ready"), 1)

            def items(todo):
                prev = None
                for it in [*todo, None]:
                    if it and it[0] == "x":
                        i = n_c[0]
                        n_c[0] += 1
                        conv_in(i, 4 * it[1] + it[2])
                        nxt = (conv_tanh, i)
                    elif it and it[0] == "z":
                        nxt = (z_tanh, it[1], it[2], z_in(it[1], it[2]))
                    elif it:
                        b = p_take()
                        p_free(act.activation(gsT[:, it[1], :], b[:, 0:NTOK], ACT.Tanh, scale=0.5))
                        nxt = None
                    else:
                        nxt = None
                    if prev:
                        prev[0](*prev[1:])
                    prev = nxt

            act.wait_ge(sem("pads_ready"), 1)
            act.wait_ge(sem("x_free"), 2)
            items([("x", 4 + j, c_) for j in range(2) for c_ in range(4)])
            act.wait_ge(sem("dtp_in"), 48)
            for lo, n in ((0, 1), (1, 2)):
                b = p_take()
                p_free(act.activation(dt[:, lo:lo + n, :], b[:, 0:64 * n].rearrange("p (t h) -> p t h", h=64), ACT.Copy))
            act.wait_ge(sem("dt_abs"), 1)
            act.activation(t_tot, tmp_a, ACT.Exp).then_inc(sem("dt_exp"), 1)
            act.activation(a_neg, a_neg, ACT.Exp).then_inc(sem("a_exp"), 1)
            act.wait_ge(sem("dt_one"), 1)
            act.activation(e_cs, cs, ACT.Ln).then_inc(sem("dt_log"), 1)
            items([("x", 0, c_) for c_ in range(4)] + [("z", 0, t) for t in range(NT)])
            act.wait_ge(sem("cs_ready"), 1)
            act.activation(e_cs, cs, ACT.Exp).then_inc(sem("exp_small"), 1)
            act.activation(e_tot, t_tot, ACT.Exp).then_inc(sem("exp_small"), 1)
            act.activation(dec_dt, tmp_a, ACT.Exp).then_inc(sem("exp_small"), 1)
            act.wait_ge(sem("lam_dot"), 1)
            act.activation(lam_t[:, 2:4], lam_t[:, 0:2], ACT.Exp).then_inc(sem("lam_exp"), 1)

            for u, (g, t) in enumerate(units):
                for d in range(2):
                    n = 2 * u + d
                    act.wait_ge(sem("d_ready"), n + 1)
                    e_ = ebuf[:, n % 4].rearrange("p h l -> p (h l)")
                    act.activation(e_, e_, ACT.Exp).then_inc(sem("e_ready"), 1)
                items(beside(g, t))
                act.wait_ge(sem("y_ready"), u + 1)
                act.activation(junk, y1[:, u % 2, :], ACT.Square, accum_out=stat[:, 36 + u % 2:37 + u % 2]).then_inc(sem("ysq_ready"), 1)

            for i in range(KT):
                b = p_take()
                if i >= 2:
                    act.wait_ge(sem("merged_ready"), i - 1)
                else:
                    act.wait_ge(sem("ssd_over"), 1)
                p_free(act.activation(proj_tmp[:, i % 2, :], b[:, 0:NTOK], ACT.Copy, scale=0.5))
            for j in range(4, 12):
                ada(j)
            for i in range(2 * A_HEADS):
                b = p_take()
                h = i % A_HEADS
                if i == 0:
                    act.wait_ge(sem("merged_ready"), KT)
                if i >= 2:
                    act.wait_ge(sem("rope_done"), i - 1)
                dst = qT[:, h, 0:P] if i < A_HEADS else kT[:, h, 0:P]
                act.activation(dst, b[:, 0:P], ACT.Copy)
                p_free(act.activation(rope_raw[:, i % 2, :], b[:, P:NTOK], ACT.Copy))
            for j in range(2):
                for t in range(NT):
                    b = p_take()
                    vb = 0 if t == 0 else t + 1
                    p_free(act.activation(vT[:, vb, j * CW:(j + 1) * CW], b[:, :], ACT.Copy))
            for i in range(KT):
                b = p_take()
                p_free(act.activation(gaT[:, i, :], b[:, 0:NTOK], ACT.Tanh, scale=0.5))
            for i in range(A_HEADS * NT):
                kn = P if i % NT == 0 else NTOK
                act.wait_ge(sem("nmax_ready"), i + 1)
                if i >= 2:
                    act.wait_ge(sem("a_ready"), i - 1)
                for m in range(2):
                    b = p_take()
                    p_free(act.activation(prob[:, i % 2, m, 0:kn], b[:, 0:kn], ACT.Exp, scale=A_HD ** -0.5,
                                          bias=neg_max[:, i % 2, m:m + 1], accum_out=row_sum[:, i % 2, m:m + 1]))
            for i in range(KT):
                b = p_take()
                if i >= 2:
                    act.wait_ge(sem("merged_ready"), KT + i - 1)
                p_free(act.activation(proj_tmp[:, i % 2, :], b[:, 0:NTOK], ACT.Copy, scale=0.5))
            act.wait_ge(sem("x_free"), AT["oTa"])
            for j in range(2):
                for t in range(NT):
                    b = p_take()
                    p_free(act.activation(y[:, t, j * CW:(j + 1) * CW], b[:, :], ACT.Copy))
            act.wait_ge(sem("p_free"), n_p[0])
            act.wait_ge(sem("attn_over"), 1)
            for t in range(NT):
                act.activation(xn[:, t, :], y[:, t, :], ACT.Square, accum_out=stat[:, 32 + t:33 + t]).then_inc(sem("sq_ready"), 1)
            for t in range(NT):
                act.wait_ge(sem("xnew_ready"), t + 1)
                act.activation(xn[:, t, :], x[:, t, :], ACT.Square, accum_out=stat[:, 32 + t:33 + t]).then_inc(sem("sq_ready"), 1)
            act.wait_ge(sem("lgm_ready"), 1)
            act.activation(lg, lg, ACT.Exp).then_inc(sem("lge_ready"), 1)
            for j in range(2):
                act.activation(route[:, 4 + j:5 + j], stat[:, 32 + j:33 + j], ACT.Copy).then_inc(sem(f"d_free{j}"), 1)
            with act.Fori(0, NE) as e:
                for j in range(4):
                    act.wait_ge(sem("gu_ready"), e * 4 + (j + 1))
                    act.wait_ge(sem(f"h_done{j % 2}"), e * 2 + (j // 2 + 1))
                    act.activation(sg[:, j % 2, :], psum[:, j % 2, 0:4 * CAP], ACT.Silu).then_inc(sem("sg_ready"), 1)
                for j in range(2):
                    act.wait_ge(sem(f"d_ready{j}"), e + 1)
                    out = psum[:, 4 + j, 0:4 * CAP].rearrange("p (a c) -> p a c", c=CAP)
                    act.activation(yT_p[:, 4 * j:4 * j + 4, bass.ds(e, 1), :].rearrange("p a b c -> p a (b c)"),
                                   out[:, :, 0:CAP_P], ACT.Copy)
                    act.activation(yT_s[:, 4 * j:4 * j + 4, bass.ds(e, 1), :].rearrange("p a b c -> p a (b c)"),
                                   out[:, :, CAP_P:CAP], ACT.Copy).then_inc(sem(f"d_free{j}"), 1)
            for t in range(NT):
                for half in range(2):
                    b = p_take()
                    p_free(act.activation(y[:, t, half * 512:(half + 1) * 512], b[:, :], ACT.Copy))
                act.wait_ge(sem("p_free"), n_p[0])
                if t:
                    act.wait_ge(sem("sq_ready"), 9 + t)
                act.activation(last_junk, y[:, t, :], ACT.Square,
                               accum_out=stat[:, 32 + t:33 + t]).then_inc(sem("sq_ready"), 1)

        @block.vector
        def _(dve):
            c = Count(dve, sem("dve_step"))
            n_x, n_t, n_c = [0], [0], [0]
            z_at = {}

            def x_take():
                n = n_x[0]
                n_x[0] += 1
                dve.wait_ge(sem("x_ready"), n + 1)
                return psum[:, 4 + n % 4]

            def x_free(ins):
                return ins.then_inc(sem("x_free"), 1)

            def link(ins):
                c.do(ins)
                c.settle()

            def x_settle():
                dve.wait_ge(sem("x_free"), n_x[0])

            def wide(v, n):
                return v.unsqueeze(2).broadcast_to([v.shape[0], v.shape[1], n])

            b = x_take()
            x_free(dve.tensor_copy(vec_a, b[:, 0:96]))
            b = x_take()
            dve.tensor_scalar(vec_b[:, 0:96], b[:, 0:96], 0.5, None, ALU.mult)
            dve.tensor_scalar(vec_b[:, 112:113], b[:, 112:113], 1.0 - LAM_INIT, None, ALU.mult)
            x_free(dve.tensor_copy(vec_b[:, 96:112], b[:, 96:112]))
            x_settle()
            dve.wait_ge(sem("cond_t"), 1)
            link(dve.tensor_scalar(junk1[:, 16:32], vec_a[:, 80:96], 0.5, None, ALU.mult))
            dve.scalar_tensor_tensor(cond.rearrange("p k c -> p c k"), junk1[:, 0:16].rearrange("p (c k) -> p c k", c=2),
                                     1.0, junk1[:, 16:32].rearrange("p (c k) -> p c k", c=2), ALU.add, ALU.mult)\
               .then_inc(sem("cond_ready"), 1)

            def normalise(out_of, src_of, m, r, signal, done, sq):
                for t in range(NT):
                    dve.wait_ge(sem("sq_ready"), sq + t + 1)
                    dve.tensor_scalar(stat[:, m + t:m + t + 1], stat[:, 32 + t:33 + t], 1.0 / D, EPS, ALU.mult, ALU.add)\
                       .then_inc(sem(signal), 1)
                for t in range(NT):
                    dve.wait_ge(sem("pow_done"), pw[0] + t + 1)
                    dve.tensor_scalar(out_of(t), src_of(t), stat[:, r + t:r + t + 1], None, ALU.mult)\
                       .then_inc(sem(done), 1)
                pw[0] += NT

            pw = [0]
            normalise(lambda t: x0[:, t, :], lambda t: x0[:, t, :], 4, 0, "ms_ready", "xn_ready", 0)

            dve.wait_ge(sem("lam_in"), 64)
            link(dve.tensor_tensor(lam_in[:, 0:4:2, :], lam_in[:, 0:4:2, :], lam_in[:, 1:4:2, :], ALU.mult))
            dve.tensor_reduce(lam_t[:, 0:2], lam_in[:, 0:4:2, :], AX.X, ALU.add).then_inc(sem("lam_dot"), 1)

            def add_bias(lo, hi):
                link(dve.tensor_tensor(mod[:, lo:hi, :], mod[:, lo:hi, :], wide(vec_a[:, lo:hi], 2), ALU.add))

            def affine(dst, sc, sh, gain):
                dve.scalar_tensor_tensor(dst[:, 0:KT, :], mod[:, sc:sc + KT, :], 1.0, wide(vec_a[:, gain:gain + KT], 2),
                                         ALU.add, ALU.mult)
                link(dve.tensor_copy(dst[:, KT:2 * KT, :], mod[:, sh:sh + KT, :]))

            dve.wait_ge(sem("p_free"), 4)
            add_bias(0, 16)
            affine(aff1, 8, 0, 48)
            dve.memset(lam_t[:, 7:8], 0.0)

            def to_cm(dst, aff):
                for k in range(KT):
                    b = x_take()
                    dve.tensor_scalar(dst[:, k, 0:P], b[:, 0:P], aff[:, k, 0:1], aff[:, KT + k, 0:1], ALU.mult, ALU.add)
                    x_free(dve.tensor_scalar(dst[:, k, P:NTOK], b[:, P:NTOK], aff[:, k, 1:2], aff[:, KT + k, 1:2],
                                             ALU.mult, ALU.add))

            to_cm(h1T, aff1)
            dve.wait_ge(sem("x_ready"), n_x[0])
            for col in (0, P + 1, PAD + 1):
                last = dve.memset(raw2[:, :, col:col + 1], 0.0)
            last.then_inc(sem("pads_ready"), 1)

            def conv_mid(i, ch):
                dve.wait_ge(sem("conv_in"), i + 1)
                r, cc = raw2[:, i % 2], conv2[:, i % 2]
                link(dve.scalar_tensor_tensor(cc, r[:, 0:PAD], vec_b[:, ch:ch + 1], cc, ALU.mult, ALU.add))
                dve.scalar_tensor_tensor(cc, r[:, 2:PAD + 2], vec_b[:, 48 + ch:49 + ch], cc, ALU.mult, ALU.add)\
                   .then_inc(sem("conv_mid"), 1)

            def conv_out(i, dst):
                dve.wait_ge(sem("t_ready"), n_t[0] + 1)
                n_t[0] += 1
                dve.scalar_tensor_tensor(dst, th[:, 0:PAD], 1.0, conv2[:, i % 2], ALU.add, ALU.mult)\
                   .then_inc(sem("t_used"), 1)

            def z_out(g, t):
                dve.wait_ge(sem("t_ready"), n_t[0] + 1)
                n_t[0] += 1
                z_ = zs2[:, g % 2, t, :]
                dve.scalar_tensor_tensor(z_, th, 1.0, z_, ALU.add, ALU.mult).then_inc(sem("t_used"), 1)
                z_at[g, t] = n_t[0]

            def items(todo):
                prev = None
                for it in [*todo, None]:
                    nxt = None
                    if it and it[0] == "x":
                        i = n_c[0]
                        n_c[0] += 1
                        conv_mid(i, 4 * it[1] + it[2])
                        nxt = (conv_out, i, BC[:, 4 * (it[1] - 4) + it[2], :] if it[1] >= 4 else xs[:, it[2], :])
                    elif it and it[0] == "z":
                        nxt = (z_out, it[1], it[2])
                    if prev:
                        prev[0](*prev[1:])
                    prev = nxt

            items([("x", 4 + j, c_) for j in range(2) for c_ in range(4)])
            dve.wait_ge(sem("p_free"), AT["dt"])
            dve.wait_ge(sem("dtp_in"), 48)
            bias3 = dt_bias.unsqueeze(1).broadcast_to([P, NT, 64])
            link(dve.tensor_tensor(dt, dt, bias3, ALU.add))
            link(dve.tensor_scalar(cs, dt, -1.0, None, ALU.mult))
            dve.tensor_tensor(tmp_a, dt, cs, ALU.min).then_inc(sem("dt_abs"), 1)
            dve.wait_ge(sem("dt_exp"), 1)
            dve.tensor_scalar(cs, t_tot, 1.0, None, ALU.add).then_inc(sem("dt_one"), 1)
            dve.wait_ge(sem("dt_one"), 1)
            link(dve.tensor_scalar(tmp_a, cs, 1.0, None, ALU.subtract))
            link(dve.tensor_scalar(dec_dt, tmp_a, 0.0, None, ALU.is_equal))
            link(dve.tensor_tensor(tmp_a, tmp_a, dec_dt, ALU.add))
            link(dve.reciprocal(tmp_a, tmp_a))
            link(dve.tensor_tensor(tmp_a, tmp_a, t_tot, ALU.mult))
            dve.wait_ge(sem("dt_log"), 1)
            link(dve.tensor_tensor(e_cs, e_cs, dec_dt, ALU.add))
            link(dve.tensor_tensor(e_cs, e_cs, tmp_a, ALU.mult))
            link(dve.scalar_tensor_tensor(dt, dt, 0.0, e_cs, ALU.max, ALU.add))
            dve.wait_ge(sem("a_exp"), 1)
            link(dve.tensor_scalar(a_neg, a_neg, -1.0, None, ALU.mult))
            dve.tensor_tensor(tmp_a, dt, a_neg.unsqueeze(1).broadcast_to([P, NT, 64]), ALU.mult).then_inc(sem("da_ready"), 1)
            items([("x", 0, c_) for c_ in range(4)] + [("z", 0, t) for t in range(NT)])
            for t in range(NT):
                b = x_take()
                x_free(dve.tensor_copy(BTM[:, t, :], b[:, :]))
            b = x_take()
            x_free(dve.tensor_copy(cs, b[:, 0:NT * 64].rearrange("p (t h) -> p t h", h=64)))
            b = x_take()
            x_free(dve.tensor_copy(t_tot, b[:, 0:NT * 64].rearrange("p (t h) -> p t h", h=64)))
            x_settle()
            for d in range(2):
                b = x_take()
                x_free(dve.tensor_copy(csT[0:32, d], b[0:32, 0:NTOK].rearrange("p (t l) -> p t l", l=P)))
            dve.wait_ge(sem("x_ready"), n_x[0])
            dve.tensor_tensor(tmp_a, t_tot, cs, ALU.subtract).then_inc(sem("cs_ready"), 1)
            dve.wait_ge(sem("exp_small"), 3)
            link(dve.tensor_tensor(dec_dt, dec_dt, dt, ALU.mult))
            dve.wait_ge(sem("lam_exp"), 1)
            link(dve.tensor_tensor(lam_t[:, 4:5], lam_t[:, 3:4], lam_t[:, 2:3], ALU.subtract))
            link(dve.tensor_scalar(lam_t[:, 4:5], lam_t[:, 4:5], LAM_INIT, None, ALU.subtract))

            def decayed(d, t, g):
                dve.tensor_tensor(xdec[:, d].rearrange("p (h e) -> p h e", e=S_HD),
                                  xTM[:, t].rearrange("p (h e) -> p h e", e=S_HD),
                                  wide(dec_dt[:, t, 32 * d + 8 * g:32 * d + 8 * g + 8], S_HD), ALU.mult)\
                   .then_inc(sem("xdec_ready"), 1)

            def mean_square(u):
                dve.wait_ge(sem("ysq_ready"), u + 1)
                dve.tensor_scalar(stat[:, 10 + u % 2:11 + u % 2], stat[:, 36 + u % 2:37 + u % 2], 1.0 / 512, EPS,
                                  ALU.mult, ALU.add).then_inc(sem("yms_ready"), 1)

            def rstd_of(u):
                dve.wait_ge(sem("pow_done"), pw[0] + 1)
                pw[0] += 1
                dve.tensor_scalar(y1[:, u % 2, :], y1[:, u % 2, :], stat[:, 8 + u % 2:9 + u % 2], None, ALU.mult)\
                   .then_inc(sem("yn_ready"), 1)

            def o_out(u):
                g, t = units[u]
                b = x_take()
                for c_ in range(4):
                    last = dve.tensor_scalar(oT[:, 4 * g + c_, t * P:(t + 1) * P], b[:, c_ * P:(c_ + 1) * P],
                                             vec_b[:, 96 + 4 * g + c_:97 + 4 * g + c_], None, ALU.mult)
                x_free(last)

            dve.wait_ge(sem("csT_out"), 16)
            for u, (g, t) in enumerate(units):
                hd = slice(S_HPG * g, S_HPG * (g + 1))
                if u:
                    mean_square(u - 1)
                if t == 0:
                    for tt in range(NT):
                        b = x_take()
                        x_free(dve.tensor_copy(xTM[:, tt, :], b[:, :]))
                    for d in range(2):
                        b = x_take()
                        x_free(dve.tensor_copy(h0T[:, d, :], b[:, :]))
                    x_settle()
                b = x_take()
                for d, tri in ((0, tri_f), (1, tri_b)):
                    last = dve.tensor_tensor(cbm[:, u % 2, d, :], b[:, 0:P], tri, ALU.mult)
                x_free(last)
                if t < 2:
                    if t == 1:
                        dve.wait_ge(sem("x_ready"), n_x[0])
                    decayed(0, t, g)
                    decayed(1, 2 * t, g)
                for d in range(2):
                    n = 2 * u + d
                    dve.wait_ge(sem(f"cs_in{n % 4}"), 16 * (n // 4 + 1))
                    for h in range(S_HPG):
                        e_ = ebuf[:, n % 4, h, :]
                        last = dve.tensor_scalar(e_, e_, cs[:, t, 32 * d + 8 * g + h:32 * d + 8 * g + h + 1], 0.0,
                                                 ALU.subtract, ALU.min)
                    last.then_inc(sem("d_ready"), 1)
                if u:
                    rstd_of(u - 1)
                x_settle()
                for d in range(2):
                    n = 2 * u + d
                    dve.wait_ge(sem("e_ready"), n + 1)
                    for h in range(S_HPG):
                        e_ = ebuf[:, n % 4, h, :]
                        last = dve.scalar_tensor_tensor(e_, e_, dt[:, t, 32 * d + 8 * g + h:32 * d + 8 * g + h + 1],
                                                        cbm[:, u % 2, d, :], ALU.mult, ALU.mult)
                    last.then_inc(sem("m_ready"), 1)
                if t == 0:
                    for d in range(2):
                        b = x_take()
                        if g:
                            dve.wait_ge(sem("stored"), 32 * g)
                        x_free(dve.tensor_copy(st_out[:, d, :], b[:, :]))
                if t == 1:
                    for d in range(2):
                        b = x_take()
                        tt = 1 + d
                        link(dve.tensor_tensor(hT1[:, d].rearrange("p (h e) -> p h e", e=S_HD),
                                               h0T[:, d].rearrange("p (h e) -> p h e", e=S_HD),
                                               wide(e_tot[:, tt, 32 * d + 8 * g:32 * d + 8 * g + 8], S_HD), ALU.mult))
                        x_free(dve.tensor_tensor(hT1[:, d], hT1[:, d], b[:, :], ALU.add))
                items(beside(g, t))
                if u:
                    o_out(u - 1)
                yv = y1[:, u % 2, :]
                yh = yv.rearrange("p (h e) -> p h e", e=S_HD)
                link(dve.tensor_tensor(yh, xTM[:, t].rearrange("p (h e) -> p h e", e=S_HD), wide(d_skip[:, hd], S_HD), ALU.mult))
                b = x_take()
                x_free(dve.tensor_tensor(yv, yv, b[:, :], ALU.add))
                x_settle()
                if t:
                    for d in range(2):
                        b = x_take()
                        x_free(dve.tensor_tensor(ytmp.rearrange("p (h e) -> p h e", e=S_HD),
                                                 b[:, :].rearrange("p (h e) -> p h e", e=S_HD),
                                                 wide(e_cs[:, t, 32 * d + 8 * g:32 * d + 8 * g + 8], S_HD), ALU.mult))
                        x_settle()
                        link(dve.tensor_tensor(yv, yv, ytmp, ALU.add))
                dve.wait_ge(sem("t_used"), z_at[g, t])
                dve.tensor_tensor(yv, yv, zs2[:, g % 2, t, :], ALU.mult).then_inc(sem("y_ready"), 1)
            mean_square(len(units) - 1)
            rstd_of(len(units) - 1)
            o_out(len(units) - 1)
            dve.wait_ge(sem("stored"), 32 * S_GROUPS)
            dve.wait_ge(sem("p_free"), AT["gs"])
            x_settle()
            dve.memset(lam_t[:, 6:7], 0.0).then_inc(sem("ssd_over"), 1)
            for i in range(KT):
                dve.wait_ge(sem("p_free"), AT["gs"] + i + 1)
                dve.scalar_tensor_tensor(mergedT[:, i, :], gsT[:, i, :], 1.0, proj_tmp[:, i % 2, :],
                                         ALU.add, ALU.mult).then_inc(sem("merged_ready"), 1)
            dve.wait_ge(sem("p_free"), AT["ada"])
            add_bias(16, 48)
            affine(aff2, 32, 24, 64)
            dve.tensor_tensor(gpost[:, 0:KT, :], mod[:, 16:24, :], wide(vec_a[:, 56:64], 2), ALU.mult)
            link(dve.tensor_tensor(gpost[:, KT:2 * KT, :], mod[:, 40:48, :], wide(vec_a[:, 72:80], 2), ALU.mult))

            for i in range(2 * A_HEADS):
                h = i % A_HEADS
                b = x_take()
                dst = qT[:, h, P:NTOK] if i < A_HEADS else kT[:, h, 2 * P:4 * P]
                c.do(dve.tensor_tensor(dst, rope_raw[:, i % 2, :], cos_t, ALU.mult))
                x_free(dve.tensor_tensor(rope_tmp, b[:, 0:2 * P], sin_t, ALU.mult))
                c.settle()
                x_settle()
                dve.tensor_tensor(dst, dst, rope_tmp, ALU.add).then_inc(sem("rope_done"), 1)
                dve.wait_ge(sem("rope_done"), i + 1)
            for j in range(2):
                b = x_take()
                x_free(dve.tensor_copy(kT[:, 4 * j:4 * j + 4, P:2 * P], b[:, :].rearrange("p (h s) -> p h s", s=P)))
            for j in range(2):
                b = x_take()
                x_free(dve.tensor_copy(k_out[:, j * 512:(j + 1) * 512], b[:, :]))

            NA = A_HEADS * NT
            keys = lambda i: P if i % NT == 0 else NTOK
            for i in range(NA + 3):
                if i < NA:
                    n = AT["attn"] + 2 * i
                    dve.wait_ge(sem("p_ready"), n + 2)
                    b0 = n % 4
                    link(dve.tensor_reduce(row_max[:, i % 2, :], psum[:, b0:b0 + 2, 0:keys(i)], AX.X, ALU.max))
                    dve.tensor_scalar(neg_max[:, i % 2, :], row_max[:, i % 2, :], -(A_HD ** -0.5), None, ALU.mult)\
                       .then_inc(sem("nmax_ready"), 1)
                if 1 <= i <= NA:
                    j = i - 1
                    n = keys(j)
                    dve.wait_ge(sem("p_free"), AT["attn"] + 2 * j + 2)
                    link(dve.reciprocal(inv_sum[:, j % 2, :], row_sum[:, j % 2, :]))
                    c.do(dve.tensor_tensor(inv_sum[:, j % 2, 1:2], inv_sum[:, j % 2, 1:2], lam_t[:, 4:5], ALU.mult))
                    link(dve.tensor_scalar(amix[:, j % 2, 0:n], prob[:, j % 2, 0, 0:n], inv_sum[:, j % 2, 0:1], None, ALU.mult))
                    dve.scalar_tensor_tensor(amix[:, j % 2, 0:n], prob[:, j % 2, 1, 0:n], inv_sum[:, j % 2, 1:2],
                                             amix[:, j % 2, 0:n], ALU.mult, ALU.add).then_inc(sem("a_ready"), 1)
                if i >= 3:
                    j = i - 3
                    dve.wait_ge(sem("pow_done"), pw[0] + 1)
                    pw[0] += 1
                    dve.tensor_scalar(o_sb[:, j % 4, :], o_sb[:, j % 4, :], stat[:, 12 + j % 4:13 + j % 4], None, ALU.mult)\
                       .then_inc(sem("on_ready"), 1)
                if 1 <= i <= NA:
                    j = i - 1
                    b = x_take()
                    x_free(dve.tensor_copy(aT[:, j % 2, 0:keys(j)], b[:, 0:keys(j)]))
                if 2 <= i <= NA + 1:
                    j = i - 2
                    b = x_take()
                    x_free(dve.tensor_copy(o_sb[:, j % 4, :], b[:, 0:P]))
                    x_settle()
                    dve.tensor_tensor_reduce(out=o_junk, in0=o_sb[:, j % 4, :], in1=o_sb[:, j % 4, :],
                                             scale=1.0 / A_VD, scalar=EPS, op0=ALU.mult, op1=ALU.add,
                                             accum_out=stat[:, 16 + j % 4:17 + j % 4]).then_inc(sem("oms_ready"), 1)
                    dve.wait_ge(sem("oms_ready"), j + 1)
                if i >= 3:
                    j = i - 3
                    h, t = divmod(j, NT)
                    b = x_take()
                    x_free(dve.tensor_scalar(oTa[:, h, t * P:(t + 1) * P], b[:, 0:P], vec_b[:, 112:113], None, ALU.mult))
            for i in range(KT):
                dve.wait_ge(sem("p_free"), AT["attn"] + 2 * NA + i + 1)
                tv = proj_tmp[:, i % 2, :]
                link(dve.scalar_tensor_tensor(tv, gaT[:, i, :], 1.0, tv, ALU.add, ALU.mult))
                dve.tensor_tensor(mergedT[:, i, :], mergedT[:, i, :], tv, ALU.add).then_inc(sem("merged_ready"), 1)

            def spread(first):
                for cnd in range(2):
                    for j in range(2):
                        for q in range(4):
                            dve.tensor_scalar(diag[:, q, :], ident, gpost[:, first + 4 * j + q, cnd:cnd + 1], None, ALU.mult)\
                               .then_inc(sem("diag_ready"), 1)
                        b = x_take()
                        x_free(dve.tensor_copy(Gb[:, cnd, j * 512:(j + 1) * 512], b[:, :]))
                x_settle()
            dve.wait_ge(sem("merged_ready"), 2 * KT)
            dve.wait_ge(sem("stored"), 32 * S_GROUPS + 32)
            spread(0)
            dve.memset(lam_t[:, 6:7], 0.0).then_inc(sem("attn_over"), 1)

            def residual(m, r, signal, done, sq):
                for t in range(NT):
                    dve.wait_ge(sem("sq_ready"), sq + t + 1)
                    dve.tensor_scalar(stat[:, m + t:m + t + 1], stat[:, 32 + t:33 + t], 1.0 / D, EPS, ALU.mult, ALU.add)\
                       .then_inc(sem(signal), 1)
                for t in range(NT):
                    dve.wait_ge(sem("pow_done"), pw[0] + t + 1)
                    link(dve.scalar_tensor_tensor(y[:, t, :], y[:, t, :], stat[:, r + t:r + t + 1],
                                                  Gb[:, min(t, 1), :], ALU.mult, ALU.mult))
                    dve.tensor_tensor(x[:, t, :], x[:, t, :], y[:, t, :], ALU.add).then_inc(sem(done), 1)
                pw[0] += NT

            dve.wait_ge(sem("x_again"), 32)
            residual(24, 20, "ms2_ready", "xnew_ready", 3)
            dve.wait_ge(sem("xnew_ready"), NT)
            normalise(lambda t: xn[:, t, :], lambda t: x[:, t, :], 4, 0, "ms3_ready", "xn2_ready", 6)
            to_cm(h2T, aff2)
            b = x_take()
            x_free(dve.tensor_copy(lg, b[:, 0:NT * NE].rearrange("p (t e) -> p t e", e=NE)))
            x_settle()
            link(dve.tensor_reduce(route[:, 0:NT], lg, AX.X, ALU.max))
            dve.tensor_tensor(lg, lg, wide(route[:, 0:NT], NE), ALU.subtract).then_inc(sem("lgm_ready"), 1)
            dve.wait_ge(sem("lge_ready"), 1)
            link(dve.tensor_reduce(route[:, 0:NT], lg, AX.X, ALU.add))
            link(dve.reciprocal(route[:, 0:NT], route[:, 0:NT]))
            dve.tensor_tensor(affin, lg, wide(route[:, 0:NT], NE), ALU.mult).then_inc(sem("affin_ready"), 1)
            b = x_take()
            x_free(dve.tensor_copy(affT[0:NE, :], b[0:NE, 0:NTOK]))
            x_settle()
            for lo, n, cap, o in ((0, P, CAP_P, 0), (P, 2 * P, CAP_S, CAP_P)):
                for r in range(cap // 8):
                    a_ = affT[0:NE, lo:lo + n]
                    m8 = mx8[0:NE, o + 8 * r:o + 8 * r + 8]
                    link(dve.max(m8, a_))
                    c.do(dve.max_index(idx_u[0:NE, o + 8 * r:o + 8 * r + 8], m8, a_))
                    c.settle()
                    link(dve.match_replace(a_, m8, a_, -1.0))
                link(dve.tensor_copy(idx_f[0:NE, o:o + cap], idx_u[0:NE, o:o + cap]))
            for i, (cap, o) in enumerate(((CAP_P, 0), (CAP_S, CAP_P))):
                n = NE * cap
                iv = idx_f[0:NE, o:o + cap].unsqueeze(1).broadcast_to([NE, NE, cap])
                if i:
                    dve.wait_ge(sem("x_ready"), n_x[0])
                dve.tensor_tensor(idx_blk[0:NE, 0:n].rearrange("p (e c) -> p e c", c=cap), iv,
                                  wide(ident[0:NE, 0:NE], cap), ALU.mult).then_inc(sem("idx_ready"), 1)
                b = x_take()
                for tt in range(1 + i):
                    dst, dg = (S_s[:, tt, :], SG_s[:, tt, :]) if i else (S_p, SG_p)
                    last = dve.tensor_scalar(dst, b[:, 0:n], iota[:, tt:tt + 1], None, ALU.is_equal)
                    if tt == i:
                        x_free(last)
                        x_settle()
                    else:
                        link(last)
                    dve.tensor_tensor(dg.rearrange("p (e c) -> p e c", c=cap), dst.rearrange("p (e c) -> p e c", c=cap),
                                      wide(affin[:, i + tt, :], cap), ALU.mult).then_inc(sem("SG_ready"), 1)
            for k in range(KT):
                for cnd, (cap, o) in enumerate(((CAP_P, 0), (CAP_S, CAP_P))):
                    b = x_take()
                    x_free(dve.tensor_scalar(xeT[:, k, :, o:o + cap], b[:, 0:NE * cap].rearrange("p (e c) -> p e c", c=cap),
                                             aff2[:, k, cnd:cnd + 1], aff2[:, KT + k, cnd:cnd + 1], ALU.mult, ALU.add))
            for j in range(5):
                b = x_take()
                x_free(dve.tensor_copy(Gt[:, j, :], b[:, 0:2 * P]))
            x_settle()
            for j in range(2):
                dve.memset(lam_t[:, 5 + j:6 + j], 0.0).then_inc(sem(f"h_done{j}"), 1)
            with dve.Fori(0, NE) as e:
                dve.tensor_copy(xe, xeT[:, :, bass.ds(e, 1), :].rearrange("p a b c -> p a (b c)")).then_inc(sem("xe_ready"), 1)
                for j in range(4):
                    dve.wait_ge(sem("sg_ready"), e * 4 + (j + 1))
                    dve.tensor_tensor(hT[:, 4 * j:4 * j + 4, :].rearrange("p a c -> p (a c)"), sg[:, j % 2, :],
                                      psum[:, 2 + j % 2, 0:4 * CAP], ALU.mult).then_inc(sem(f"h_done{j % 2}"), 1)
            for j in range(6):
                for kk in range(2):
                    b = x_take()
                    x_free(dve.tensor_copy(ye[:, j, kk * 512:(kk + 1) * 512], b[:, :]))
            spread(KT)
            residual(24, 20, "ms4_ready", "out_ready", 9)

    return nc


def kernel(**inputs):
    import numpy as _np
    import concourse.bacc as _bacc
    from concourse import mybir as _mybir
    from concourse.bass_utils import run_bass_kernel_spmd as _run

    names = ["x_prompt", "x_sample", "cache_k", "cache_v", "state_ssd", "c", "c_ctx", "w_ada", "b_ada",
             "g_pre_mix", "g_post_mix", "g_pre_ffn", "g_post_ffn", "w_in", "lam_q1", "lam_k1", "lam_q2", "lam_k2",
             "w_subln", "conv_w", "conv_b", "dt_bias", "a_log", "d_skip", "w_ssd_norm", "w_o_attn", "w_o_ssd",
             "w_out", "w_router", "w_gate", "w_up", "w_down"]
    nc = _bacc.Bacc("TRN2", target_bir_lowering=False, num_devices=1)
    arrays, t_in, t_out = {}, {}, {}
    f32 = _mybir.dt.float32
    for name in names:
        a = _np.ascontiguousarray(inputs[name])
        arrays["in_" + name] = a
        t_in[name] = nc.dram_tensor("in_" + name, a.shape, f32, kind="ExternalInput").ap()
    arrays["shape_consts"] = shape_constants()
    consts = nc.dram_tensor("shape_consts", (P, C_END), f32, kind="ExternalInput").ap()
    outs = {"xp": (1, P, D), "xs": (1, 2 * P, D), "k": (1, 1, P, A_HEADS, 2 * A_HD),
            "v": (1, 1, P, A_HEADS, A_VD), "state": (1, 1, 2, S_HEADS, S_HD, S_STATE)}
    for name, shape in outs.items():
        t_out[name] = nc.dram_tensor("out_" + name, shape, f32, kind="ExternalOutput").ap()
    scratch = nc.dram_tensor("cs_rows", (2, NT, S_HEADS, P), f32, kind="Internal").ap()
    build(nc, t_in, t_out, consts, scratch)
    r = _run(nc, [arrays], core_ids=[0])
    return tuple(r.results[0]["out_" + name] for name in outs)
```

```python
import math
from contextlib import ExitStack

import numpy as np

import concourse.bass as bass
from concourse import mybir

F32 = mybir.dt.float32
U32 = mybir.dt.uint32
ALU = mybir.AluOpType
ACT = mybir.ActivationFunctionType
AX = mybir.AxisListType

P = 128
NT = 3
NTOK = NT * P
D = 1024
KT = D // P
EPS = 1e-6
CW = 512
A_HEADS, A_HD, A_VD = 8, 64, 128
S_INNER, S_HEADS, S_HD, S_GROUPS, S_STATE = 2048, 32, 64, 4, 128
S_HPG = S_HEADS // S_GROUPS
NE, CAP_P, CAP_S, D_FF = 16, 16, 32, 2048
CAP = CAP_P + CAP_S
HALF = P // 2
GE = 4
LAM_INIT = 0.8 - 0.6 * math.exp(-0.3 * 0)
Q0, K0, V0 = 0, 1024, 2048
Z0, X0, B0, C0 = 3072, 5120, 7168, 7680
DT0, GA0, GS0 = 8192, 8256, 9280
PAD = NTOK + 1
TOK = (0, P + 1, 2 * P + 1)
FF_SLOTS = 6

C_ID, C_TF, C_TB, C_PM, C_ON, C_COS, C_SIN, C_IO, C_SEL, C_END = 0, 128, 256, 384, 512, 640, 896, 1152, 1154, 1156


def shape_constants():
    c = np.zeros((P, C_END), np.float32)
    i = np.arange(P)
    c[:, C_ID:C_ID + P] = np.eye(P)
    c[:, C_TF:C_TF + P] = i[:, None] <= i[None, :]
    c[:, C_TB:C_TB + P] = i[:, None] >= i[None, :]
    half, nf = A_HD // 2, A_HD // 4
    for d in range(P):
        if d % half < nf:
            c[d + nf, C_PM + d] = -1.0
        else:
            c[d - nf, C_PM + d] = 1.0
    c[:, C_ON:C_ON + P] = 1.0
    tok = np.arange(2 * P)
    pos = np.stack([tok // 64, tok % 64]).astype(np.float32)
    inv = np.power(np.float32(10000.0), -np.arange(nf, dtype=np.float32) / np.float32(nf)).astype(np.float32)
    axis = (i % A_HD) // half
    ang = pos[axis] * inv[i % nf][:, None]
    c[:, C_COS:C_COS + 2 * P] = np.cos(ang.astype(np.float32))
    c[:, C_SIN:C_SIN + 2 * P] = np.sin(ang.astype(np.float32))
    c[:, C_IO] = i
    c[:, C_IO + 1] = i + P
    for j in range(2):
        c[:, C_SEL + j] = i % 32 == j
    return c


class Count:

    def __init__(self, eng, sem):
        self.eng, self.sem, self.n = eng, sem, 0

    def do(self, ins):
        self.n += 1
        return ins.then_inc(self.sem, 1)

    def settle(self):
        self.eng.wait_ge(self.sem, self.n)


def build(nc, t_in, t_out, consts, scratch):
    ctx = ExitStack()
    with ctx:
        arena = ctx.enter_context(nc.sbuf_tensor("arena", [P, 53184], F32))
        psum = ctx.enter_context(nc.psum_tensor("psum", [P, 8, 512], F32))
        sems = {}

        def sem(name):
            if name not in sems:
                sems[name] = ctx.enter_context(nc.semaphore(name))
            return sems[name]

        def at(kib, *shape):
            n = int(np.prod(shape))
            off = int(kib * 256)
            assert off + n <= 53184, (kib, shape)
            v = arena[:, off:off + n]
            if len(shape) == 1:
                return v
            names = "abcd"[:len(shape)]
            return v.rearrange(f"p ({' '.join(names)}) -> p {' '.join(names)}",
                               **{k: s for k, s in zip(names[1:], shape[1:])})

        slots = [at(16 * s, KT, CW) for s in range(FF_SLOTS)]
        cst = at(96, C_END)
        ident, tri_f, tri_b = cst[:, C_ID:C_ID + P], cst[:, C_TF:C_TF + P], cst[:, C_TB:C_TB + P]
        perm, ones = cst[:, C_PM:C_PM + P], cst[:, C_ON:C_ON + P]
        cos_t, sin_t = cst[:, C_COS:C_COS + 2 * P], cst[:, C_SIN:C_SIN + 2 * P]
        iota = cst[:, C_IO:C_IO + 2]
        cond_rows = cst[:, C_SEL:C_SEL + 2]
        sm = [101.0]

        def small(*shape):
            v = at(sm[0], *shape)
            sm[0] += int(np.prod(shape)) / 256
            assert sm[0] <= 109
            return v

        vec_a = small(96)
        vec_b = small(113)
        cond = at(109, KT, 32)
        mod = small(48, 2)
        aff1 = small(2 * KT, 2)
        aff2 = small(2 * KT, 2)
        gpost = small(2 * KT, 2)
        dt_w = at(203.5, KT, 64)
        dt_bias, a_neg = small(64), small(64)
        d_skip = small(S_HEADS)
        dt, cs, e_cs, dec_dt = small(NT, 64), small(NT, 64), small(NT, 64), small(NT, 64)
        e_tot, t_tot, tmp_a = small(NT, 64), small(NT, 64), small(NT, 64)
        lam_in, lam_t = at(58, 4, A_HD), small(8)
        stat = small(48)
        neg_max, row_max, row_sum, inv_sum = small(2, 2), small(2, 2), small(2, 2), small(2, 2)
        route = small(8)
        h1T = at(110, KT, NTOK)
        mergedT = at(122, KT, NTOK)
        x0 = at(32, NT, D)
        rows_a, rows_b = at(44, P), at(44.5, P)
        junk0, junk1 = at(46, D), at(50, D)
        raw2 = at(32, 2, PAD + 2)
        conv2 = at(35.25, 2, PAD)
        th = at(38.5, 512)
        xs = at(40.5, 4, PAD)
        xTM = at(46.75, NT, 512)
        zs2 = at(52.75, 2, NT, 512)
        h0raw = at(64.75, 2, 4, P)
        h0T = at(68.75, 2, 512)
        hT1 = at(72.75, 2, 512)
        xdec = at(76.75, 2, 512)
        y1 = at(80.75, 2, 512)
        ytmp = at(84.75, 512)
        junk = at(86.75, 512)
        cbm = at(88.75, 2, 2, P)
        st_out = at(90.75, 2, 512)
        BC = at(134, 8, PAD)
        BTM = at(146.25, NT, 512)
        oT = at(152.25, 16, NTOK)
        csT = at(152.25, 2, NT, P)
        ebuf = at(176.25, 4, S_HPG, P)
        gsT = at(192.25, KT, NTOK)
        qT = at(134, A_HEADS, NTOK)
        kT = at(146, A_HEADS, 512)
        vT = at(162, 4, D)
        oTa = at(178, A_HEADS, NTOK)
        gaT = at(190, KT, NTOK)
        k_out = at(202, D)
        rope_raw = at(64, 2, 2 * P)
        rope_tmp = at(66, 2 * P)
        ck_raw = at(67, D)
        prob = at(71, 2, 2, NTOK)
        amix = at(77, 2, NTOK)
        aT = at(80, 2, NTOK)
        o_sb = at(83, 4, P)
        o_junk = at(85, P)
        proj_tmp = at(86, 2, NTOK)
        x = at(110, NT, D)
        hT = at(122, 16, HALF)
        xe = at(126, KT, HALF)
        wr = at(198.5, KT, NE)
        lg, affin = at(194, NT, NE), at(194.25, NT, NE)
        affT = at(129, NTOK)
        idx_u, idx_f = at(132, CAP).bitcast(U32), at(132.25, CAP)
        mx8 = at(132.5, CAP)
        y = at(134, NT, D)
        S_p, S_s = at(134, NE * CAP_P), at(135, 2, NE * CAP_S)
        SG_s = at(139, 2, NE * CAP_S)
        SG_p = at(143, NE, CAP_S)
        xn = at(146, NT, D)
        h2T = at(158, KT, NTOK)
        idx_blk = at(158, NE * CAP_S)
        stage_s, stage_p = at(146, D), at(150, D)
        h_sb = at(156, 2, 2 * P)
        sg = at(158, 2, 2 * P)
        Gs_cur, Gp_cur = at(160, 2 * P), at(161, P)
        Gt_p, Gt_s = at(164, 4, P), at(166, 4, 2 * P)
        xeT = at(170, KT, NE, CAP)
        Gb = at(199, 2, D)
        diag = at(194.5, 2, 4, P)
        mod_rows = at(89.25, 2, CW)
        last_junk = at(32, D)

        w_in, w_ada = t_in["w_in"][0], t_in["w_ada"][0]

        def cols(w, c, k=0):
            return w[k * D:(k + 1) * D, c:c + CW].rearrange("(k p) n -> p k n", p=P)

        chunks = []

        def add(w, c, k=0):
            chunks.append(cols(w, c, k))

        for j in range(4):
            add(w_ada, j * CW)
        add(w_in, B0)
        add(w_in, C0)
        for g in range(S_GROUPS):
            add(w_in, X0 + g * CW)
            add(w_in, Z0 + g * CW)
        for j in range(2):
            add(w_in, GS0 + j * CW)
        for j in range(2):
            for k in range(2):
                add(t_in["w_o_ssd"][0], j * CW, k)
        for c in (Q0, K0, V0, GA0):
            for j in range(2):
                add(w_in, c + j * CW)
        for j in range(4, 12):
            add(w_ada, j * CW)
        for w in ("w_o_attn", "w_out"):
            for j in range(2):
                add(t_in[w][0], j * CW)
        NM = len(chunks)
        assert NM % 2 == 0
        AT = {}

        units = [(g, t) for g in range(S_GROUPS) for t in range(NT)]

        def beside(g, t):
            if g + 1 < S_GROUPS:
                return [[("x", g + 1, 0), ("x", g + 1, 1)], [("x", g + 1, 2), ("x", g + 1, 3)],
                        [("z", g + 1, 0), ("z", g + 1, 1), ("z", g + 1, 2)]][t]
            return [[("g", i) for i in range(3)], [("g", i) for i in range(3, 6)], [("g", 6), ("g", 7)]][t]

        beside_attn = {2 + 3 * n: p for n, p in enumerate(
            [[("ga", 2 * n), ("ga", 2 * n + 1)] for n in range(4)] + [[("ada", 2 * n), ("ada", 2 * n + 1)] for n in range(2, 6)])}

        block = ctx.enter_context(nc.Block())

        @block.tensor
        def _(pe):
            n_p, n_x, n_w, n_t = [0], [0], [0], [0]
            AT["chunk_end"] = []

            def p_written():
                pe.wait_ge(sem("p_free"), n_p[0])

            def x_written():
                pe.wait_ge(sem("x_free"), n_x[0])

            def p_bank(k=1):
                n = n_p[0]
                n_p[0] += k
                if n + k > 4:
                    pe.wait_ge(sem("p_free"), n + k - 4)
                return psum[:, n % 4] if k == 1 else None

            def p_done(mm):
                mm.then_inc(sem("p_ready"), 1)

            def x_bank():
                n = n_x[0]
                n_x[0] += 1
                if n >= 4:
                    pe.wait_ge(sem("x_free"), n - 3)
                return psum[:, 4 + n % 4]

            def x_done(mm):
                mm.then_inc(sem("x_ready"), 1)

            def chunk():
                n = n_w[0]
                n_w[0] += 1
                pe.wait_ge(sem(f"w_in_slot{n % 2}"), 16 * (n // 2 + 1))
                return slots[n % 2]

            def chunk_used():
                AT["chunk_end"].append(("p_ready", n_p[0]))

            def cm_tile(w, ct, src=None, last=False):
                src = h1T if src is None else src
                b = p_bank()
                for k in range(KT):
                    mm = pe.matmul(b[:, 0:NTOK], w[:, k, ct * P:(ct + 1) * P], src[:, k, :],
                                   start=k == 0, stop=k == KT - 1)
                p_done(mm)
                if last:
                    chunk_used()

            def tm_tile(w, t, src=None, last=False):
                src = h1T if src is None else src
                b = p_bank()
                for k in range(KT):
                    mm = pe.matmul(b[:, :], src[:, k, t * P:(t + 1) * P], w[:, k, :],
                                   start=k == 0, stop=k == KT - 1)
                p_done(mm)
                if last:
                    chunk_used()

            def ada():
                w = chunk()
                b = p_bank()
                for k in range(KT):
                    q = k % 4
                    mm = pe.matmul(b[32 * q:32 * q + 32, :], cond[:, k, :], w[:, k, :], start=k < 4, stop=k >= 4,
                                   tile_position=(0, 32 * q))
                p_done(mm)
                chunk_used()
                ada_at.append(n_p[0])

            def ada_cm(j):
                pe.wait_ge(sem("p_free"), ada_at[j])
                b = x_bank()
                for ct in range(4):
                    mm = pe.matmul(b[:, 2 * ct:2 * ct + 2], mod_rows[:, j % 2, ct * P:(ct + 1) * P], cond_rows,
                                   start=True, stop=True)
                x_done(mm)
                AT["ada_x"].append(n_x[0])

            ada_at = []
            AT["ada_x"] = []

            def transposes(pairs):
                b = x_bank()
                at_ = 0
                for src in pairs:
                    rows, width = src.shape[0], int(np.prod(src.shape[1:]))
                    mm = pe.transpose(b[0:width, at_:at_ + rows], src, ident[0:rows, 0:rows])
                    at_ += rows
                x_done(mm)

            pe.wait_ge(sem("const_in"), 16)
            pe.wait_ge(sem("rows_a_in"), 16 * 7)
            transposes([rows_a[0:96, :]])
            pe.wait_ge(sem("rows_b_in"), 16 * 4)
            transposes([rows_b[0:113, :]])
            pe.wait_ge(sem("cond_ready"), 1)
            for j in range(4):
                ada()
                if j:
                    ada_cm(j - 1)
            ada_cm(3)
            pe.wait_ge(sem("xn_ready"), NT)
            for k in range(KT):
                transposes([x0[:, t, k * P:(k + 1) * P] for t in range(NT)])
            x_written()
            for _ in range(2):
                w = chunk()
                for ct in range(4):
                    cm_tile(w, ct, last=ct == 3)
            n_t[0] += 8
            after_bc = n_t[0]
            pe.wait_ge(sem("dtw_in"), 16)
            for ts in ((0,), (1, 2)):
                b = p_bank()
                for i, t in enumerate(ts):
                    for k in range(KT):
                        mm = pe.matmul(b[:, i * 64:(i + 1) * 64], h1T[:, k, t * P:(t + 1) * P], dt_w[:, k, :],
                                       start=k == 0, stop=k == KT - 1)
                p_done(mm)
            AT["dt"] = n_p[0]
            w = chunk()
            for ct in range(4):
                cm_tile(w, ct, last=ct == 3)
            w = chunk()
            for t in range(NT):
                tm_tile(w, t, last=t == 2)
            x_items = {0: n_t[0] + 4}
            n_t[0] += 7
            pe.wait_ge(sem("t_used"), after_bc)
            for t in range(NT):
                transposes([BC[:, g, TOK[t]:TOK[t] + P] for g in range(4)])
            btm_at = n_x[0]
            pe.wait_ge(sem("da_ready"), 1)
            b = x_bank()
            for t in range(NT):
                pe.matmul(b[:, t * 64:t * 64 + 32], tri_f, tmp_a[:, t, 0:32], start=True, stop=True)
                mm = pe.matmul(b[:, t * 64 + 32:t * 64 + 64], tri_b, tmp_a[:, t, 32:64], start=True, stop=True)
            x_done(mm)
            b = x_bank()
            mm = pe.matmul(b[:, 0:NT * 64], ones, tmp_a[:, :, :], start=True, stop=True)
            x_done(mm)
            for d, tri in ((0, tri_f), (1, tri_b)):
                b = x_bank()
                for t in range(NT):
                    mm = pe.matmul(b[0:32, t * P:(t + 1) * P], tmp_a[:, t, 32 * d:32 * d + 32], tri,
                                   start=True, stop=True)
                x_done(mm)

            AT["csT"] = n_x[0]

            w = None

            def side(item):
                nonlocal w
                if item[0] != "g":
                    n_t[0] += 1
                if item[0] == "x":
                    x_items[item[1]] = n_t[0]
                if item[0] == "x":
                    if item[2] == 0:
                        w = chunk()
                    cm_tile(w, item[2], last=item[2] == 3)
                elif item[0] == "z":
                    if item[2] == 0:
                        w = chunk()
                    tm_tile(w, item[2], last=item[2] == 2)
                else:
                    if item[1] % 4 == 0:
                        w = chunk()
                    cm_tile(w, item[1] % 4, last=item[1] % 4 == 3)

            def back_to_cm(u):
                pe.wait_ge(sem("yn_ready"), u + 1)
                transposes([y1[:, u % 2, c * P:(c + 1) * P] for c in range(4)])

            for u, (g, t) in enumerate(units):
                if t == 0:
                    pe.wait_ge(sem("t_used"), x_items[g])
                    for tt in range(NT):
                        transposes([xs[:, c, TOK[tt]:TOK[tt] + P] for c in range(4)])
                    for d in range(2):
                        pe.wait_ge(sem(f"h0_in_d{d}"), 16 * (g + 1))
                        transposes([h0raw[:, d, c, :] for c in range(4)])
                    AT.setdefault("h0", []).append(n_x[0])
                b = x_bank()
                mm = pe.matmul(b[:, 0:P], BC[:, g, TOK[t]:TOK[t] + P], BC[:, 4 + g, TOK[t]:TOK[t] + P],
                               start=True, stop=True)
                x_done(mm)
                first, *others = beside(g, t)
                side(first)
                if t == 0:
                    for d in range(2):
                        pe.wait_ge(sem("xdec_ready"), 4 * g + d + 1)
                        pe.wait_ge(sem("x_free"), btm_at)
                        b = x_bank()
                        for c in range(4):
                            mm = pe.matmul(b[:, c * P:(c + 1) * P], xdec[:, d, c * P:(c + 1) * P],
                                           BTM[:, 0, g * P:(g + 1) * P], start=True, stop=True)
                        x_done(mm)
                        AT.setdefault("st", []).append(n_x[0])
                if t == 1:
                    for d in range(2):
                        pe.wait_ge(sem("xdec_ready"), 4 * g + 2 + d + 1)
                        b = x_bank()
                        mm = pe.matmul(b[:, :], BTM[:, 1 + d, g * P:(g + 1) * P], xdec[:, d, :],
                                       start=True, stop=True)
                        x_done(mm)
                    hT1_at = n_x[0]
                for item in others:
                    side(item)
                if u:
                    back_to_cm(u - 1)
                pe.wait_ge(sem("m_sum"), u + 1)
                b = x_bank()
                AT.setdefault("y", []).append(n_x[0])
                for h in range(S_HPG):
                    o = b[:, h * S_HD:(h + 1) * S_HD]
                    xh = xTM[:, t, h * S_HD:(h + 1) * S_HD]
                    mm = pe.matmul(o, ebuf[:, (2 * u) % 4, h, :], xh, start=True, stop=True)
                x_done(mm)
                if t:
                    if t == 1:
                        pe.wait_ge(sem("x_free"), hT1_at)
                    for d in range(2):
                        fresh = (t == 1) == (d == 0)
                        b = x_bank()
                        mm = pe.matmul(b[:, :], BC[:, 4 + g, TOK[t]:TOK[t] + P],
                                       h0T[:, d, :] if fresh else hT1[:, d, :], start=True, stop=True)
                        x_done(mm)
            back_to_cm(len(units) - 1)

            AT["gs"] = n_p[0]
            x_written()
            for j in range(2):
                n0 = n_p[0]
                p_bank(4)
                for k2 in range(2):
                    w = chunk()
                    for ct in range(4):
                        for k in range(KT):
                            mm = pe.matmul(psum[:, (n0 + ct) % 4, 0:NTOK], w[:, k, ct * P:(ct + 1) * P],
                                           oT[:, k2 * KT + k, :], start=k2 == 0 and k == 0,
                                           stop=k2 == 1 and k == KT - 1)
                        if k2 == 1:
                            p_done(mm)
                    if k2 == 1:
                        chunk_used()
                    else:
                        mm.then_inc(sem("half_used"), 1)
                        AT["chunk_end"].append(("half_used", j + 1))

            def rope(i):
                pe.wait_ge(sem("p_free"), AT["q"] + i + 1)
                b = x_bank()
                x_done(pe.matmul(b[:, 0:2 * P], perm, rope_raw[:, i % 2, :], start=True, stop=True))

            AT["q"] = n_p[0]
            for i in range(2 * A_HEADS):
                if i % 4 == 0:
                    w = chunk()
                cm_tile(w, i % 4, last=i % 4 == 3)
                if i:
                    rope(i - 1)
            rope(2 * A_HEADS - 1)
            pe.wait_ge(sem("ck_in"), 16)
            for j in range(2):
                transposes([ck_raw[:, (4 * j + c) * P:(4 * j + c + 1) * P] for c in range(4)])
            AT["ck"] = n_x[0]
            p_written()
            for j in range(2):
                transposes([kT[:, 4 * j + c, 0:P] for c in range(4)])
                AT.setdefault("kout", []).append(n_x[0])
            for _ in range(2):
                w = chunk()
                for t in range(NT):
                    tm_tile(w, t, last=t == 2)
            AT["v"] = n_p[0]
            pairs = [(h, t) for h in range(A_HEADS) for t in range(NT)]
            NA = len(pairs)
            assert n_p[0] % 2 == 0
            AT["attn"] = n_p[0]
            pe.wait_ge(sem("rope_done"), 2 * A_HEADS)
            pe.wait_ge(sem("x_free"), AT["ck"])
            pe.wait_ge(sem("p_free"), AT["v"])
            aT_at = []
            pe.wait_ge(sem("cv_in"), 16)

            def key_blocks(t):
                return [(0, 0)] if t == 0 else [(b_, b_ + 1) for b_ in range(3)]

            def scores(i):
                h, t = pairs[i]
                k0, kn = (0, P) if t == 0 else (P, NTOK)
                n = n_p[0]
                AT.setdefault("scores", []).append(n)
                p_bank(2)
                for m in range(2):
                    r = slice(m * A_HD, (m + 1) * A_HD)
                    mm = pe.matmul(psum[:, (n + m) % 4, 0:kn], qT[r, h, t * P:(t + 1) * P],
                                   kT[r, h, k0:k0 + kn], start=True, stop=True)
                    p_done(mm)

            late = []

            scores(0)
            for i in range(NA + 5):
                if i + 1 < NA:
                    scores(i + 1)
                for j in late:
                    ada_cm(j)
                late = []
                for kind, n in beside_attn.get(i, []):
                    if kind == "ga":
                        if n % 4 == 0:
                            w = chunk()
                        cm_tile(w, n % 4, last=n % 4 == 3)
                    else:
                        ada()
                        late.append(n)
                if 2 <= i <= NA + 1:
                    h, t = pairs[i - 2]
                    pe.wait_ge(sem("a_ready"), i - 1)
                    transposes([amix[:, i % 2, c * P:(c + 1) * P] for c, _ in key_blocks(t)])
                    aT_at.append(n_x[0])
                if 3 <= i <= NA + 2:
                    h, t = pairs[i - 3]
                    pe.wait_ge(sem("x_free"), aT_at[i - 3])
                    b = x_bank()
                    kb = key_blocks(t)
                    for c, vb in kb:
                        mm = pe.matmul(b[:, 0:P], aT[:, (i - 3) % 2, c * P:(c + 1) * P],
                                       vT[:, vb, h * P:(h + 1) * P], start=c == 0, stop=c == len(kb) - 1)
                    x_done(mm)
                if i >= 5:
                    pe.wait_ge(sem("on_ready"), i - 4)
                    transposes([o_sb[:, (i - 5) % 4, :]])
            AT["attn_end"] = n_p[0]

            AT["oTa"] = n_x[0]
            x_written()
            for _ in range(2):
                w = chunk()
                for ct in range(4):
                    cm_tile(w, ct, src=oTa, last=ct == 3)
            pe.wait_ge(sem("merged_ready"), 2 * KT)

            def spread(n):
                b = x_bank()
                for q in range(4):
                    pe.wait_ge(sem("diag_ready"), 4 * n + q + 1)
                    mm = pe.matmul(b[:, q * P:(q + 1) * P], ones, diag[:, n % 2, q, :], start=True, stop=True)
                x_done(mm)
            def x_to_cm(t):
                pe.wait_ge(sem("xn2_ready"), t + 1)
                for j in range(2):
                    transposes([xn[:, t, k * P:(k + 1) * P] for k in range(4 * j, 4 * j + 4)])
                h2_at.append(n_x[0])

            def router(t):
                pe.wait_ge(sem("x_free"), h2_at[t])
                b = x_bank()
                for k in range(KT):
                    mm = pe.matmul(b[:, 0:NE], h2T[:, k, t * P:(t + 1) * P], wr[:, k, :], start=k == 0, stop=k == KT - 1)
                x_done(mm)

            h2_at = []
            w_o = []

            def mixer_out(t):
                for j in range(2):
                    tm_tile(w_o[j], t, src=mergedT, last=t == 2)

            for j in range(2):
                w_o.append(chunk())
                tm_tile(w_o[j], 0, src=mergedT)
                spread(2 * j)
                spread(2 * j + 1)
            mixer_out(1)
            x_to_cm(0)
            mixer_out(2)
            pe.wait_ge(sem("wr_in"), 16)
            router(0)
            x_to_cm(1)
            router(1)
            x_to_cm(2)
            router(2)
            pe.wait_ge(sem("affin_ready"), 1)
            transposes([affin[:, t, :] for t in range(NT)])
            for n in range(4):
                pe.wait_ge(sem("diag2_ready"), 4 * (n + 1))
                b = p_bank()
                for q in range(4):
                    mm = pe.matmul(b[:, q * P:(q + 1) * P], ones, diag[:, n % 2, q, :], start=True, stop=True)
                p_done(mm)
            for i, n in ((0, NE * CAP_P), (1, NE * CAP_S)):
                pe.wait_ge(sem("idx_ready"), i + 1)
                b = x_bank()
                x_done(pe.matmul(b[:, 0:n], ones[0:NE, :], idx_blk[0:NE, 0:n], start=True, stop=True))
            x_written()
            for k in range(KT):
                b = x_bank()
                x_done(pe.matmul(b[:, 0:NE * CAP_P], xn[:, 0, k * P:(k + 1) * P], S_p, start=True, stop=True))
                b = x_bank()
                pe.matmul(b[:, :], xn[:, 1, k * P:(k + 1) * P], S_s[:, 0, :], start=True, stop=False)
                x_done(pe.matmul(b[:, :], xn[:, 2, k * P:(k + 1) * P], S_s[:, 1, :], start=False, stop=True))
                if k == KT // 2:
                    pe.wait_ge(sem("SG_ready"), NT)
                    for j in range(NE // GE):
                        transposes([SG_s[:, t, j * P:(j + 1) * P] for t in range(2)])
                    transposes([SG_p[:, GE * j:GE * (j + 1), :].rearrange("p e c -> p (e c)") for j in range(NE // GE)])
            AT["dispatched"] = n_x[0]

            x_written()
            p_written()
            with pe.Fori(0, NE // GE) as g:
                for i in range(GE):
                    pe.wait_ge(sem("xe_ready"), g * GE + (i + 1))

                    def h_to_cm(j):
                        pe.wait_ge(sem("h_done"), g * 16 + (4 * i + j + 3))
                        pe.wait_ge(sem("hT_done"), g * 16 + (4 * i + j + 1))
                        if i == 0 and j == 0:
                            pe.wait_ge(sem("comb_done"), g * 6 + 2)
                        for a in range(2):
                            mm = pe.transpose(psum[:, 4, a * P:(a + 1) * P], h_sb[:, j % 2, a * P:(a + 1) * P], ident)
                        mm.then_inc(sem("hT_psum"), 1)

                    for c in range(12):
                        s = (c + 2) % FF_SLOTS
                        if c == 8:
                            h_to_cm(3)
                            pe.wait_ge(sem("hT_done"), g * 16 + (4 * i + 5))
                        pe.wait_ge(sem(f"ff_slot{s}"), g * 128 + (32 * i + 16 * (c // 6 + 1)))
                        w = slots[s]
                        if c < 8:
                            j, up = c // 2, c % 2
                            bank, src, k0 = 2 * up + j % 2, xe, 0
                            if not up:
                                pe.wait_ge(sem("h_done"), g * 16 + (4 * i + j + 1))
                        else:
                            j, up = (c - 8) // 2, c % 2
                            bank, src, k0 = 5 + j, hT, KT * up
                            if not up:
                                pe.wait_ge(sem(f"d_free{j}"), g * GE + (i + 1))
                        first, last = c < 8 or not up, c < 8 or up
                        for k in range(KT):
                            for q in range(2):
                                mm = pe.matmul(psum[HALF * q:HALF * (q + 1), bank, 0:2 * P], src[:, k0 + k, :],
                                               w[:, k, 2 * P * q:2 * P * (q + 1)], start=bool(first and k == 0),
                                               stop=bool(last and k == KT - 1), tile_position=(0, HALF * q))
                        if c < 8:
                            mm.then_inc(sem("gu_ready" if up else "ff_used"), 1)
                            if up and j:
                                h_to_cm(j - 1)
                        else:
                            mm.then_inc(sem(f"d_ready{j}" if up else "ff_used"), 1)
                pe.wait_ge(sem("Gcur_ready"), g + 1)
                for j in range(2):
                    pe.wait_ge(sem(f"d_free{j}"), g * GE + (GE + 1))
                pe.wait_ge(sem("hT_done"), g * 16 + 17)
                for n, (t, half) in enumerate([(t, half) for t in range(NT) for half in range(2)]):
                    pe.wait_ge(sem("comb_done"), g * 6 + (n + 1))
                    bank = (7, 4)[n % 2]
                    cols_ = slice(half * CW, (half + 1) * CW)
                    if t:
                        mm = pe.matmul(psum[:, bank, :], Gs_cur[:, (t - 1) * P:t * P], stage_s[:, cols_], start=True, stop=True)
                    else:
                        mm = pe.matmul(psum[:, bank, :], Gp_cur, stage_p[:, cols_], start=True, stop=True)
                    mm.then_inc(sem("comb_ready"), 1)

        @block.sync
        def _(sp):
            sp.dma_start(cst, consts).then_inc(sem("const_in"), 16)
            for n, src in enumerate(chunks):
                if n >= 2:
                    name, value = AT["chunk_end"][n - 2]
                    sp.wait_ge(sem(name), value)
                sp.dma_start(slots[n % 2], src).then_inc(sem(f"w_in_slot{n % 2}"), 16)
            wg, wu, wd = t_in["w_gate"][0], t_in["w_up"][0], t_in["w_down"][0]

            def expert_chunk(e, c):
                w, c0, k0 = ((wg, wu)[c % 2], c // 2, 0) if c < 8 else (wd, (c - 8) // 2, c % 2)
                return w[e, k0 * D:(k0 + 1) * D, c0 * CW:(c0 + 1) * CW].rearrange("(k p) n -> p k n", p=P)

            def load(e, c):
                s = (c + 2) % FF_SLOTS
                sp.dma_start(slots[s], expert_chunk(e, c)).then_inc(sem(f"ff_slot{s}"), 16)

            def wait_used(e, c):
                if c >= 8 and c % 2:
                    sp.wait_ge(sem(f"d_ready{(c - 8) // 2}"), e + 1)
                elif c % 2:
                    sp.wait_ge(sem("gu_ready"), e * 4 + (c // 2 + 1))
                else:
                    sp.wait_ge(sem("ff_used"), e * 6 + (c // 2 + 1))

            for c in range(12):
                if c == 0:
                    sp.wait_ge(sem("ssd_over"), 1)
                if c == 2:
                    sp.wait_ge(sem("attn_over"), 1)
                if c == 4:
                    sp.wait_ge(sem("p_ready"), AT["chunk_end"][NM - 1][1])
                if c >= 6:
                    wait_used(0, c - 6)
                load(0, c)
            with sp.Fori(1, NE) as e:
                for c in range(12):
                    wait_used(e - 1 if c < 6 else e, (c - 6) % 12)
                    load(e, c)

        n_store = [0]

        @block.gpsimd
        def _(pool):
            pool.dma_start(dt_bias, t_in["dt_bias"][0].rearrange("a h -> (a h)").partition_broadcast(P)).then_inc(sem("dtp_in"), 16)
            pool.dma_start(a_neg, t_in["a_log"][0].rearrange("a h -> (a h)").partition_broadcast(P)).then_inc(sem("dtp_in"), 16)
            pool.dma_start(d_skip, t_in["d_skip"][0].partition_broadcast(P)).then_inc(sem("dtp_in"), 16)
            for i, name in enumerate(("lam_q1", "lam_k1", "lam_q2", "lam_k2")):
                pool.dma_start(lam_in[:, i, :], t_in[name][0].partition_broadcast(P)).then_inc(sem("lam_in"), 16)
            pool.dma_start(dt_w, w_in[:, DT0:DT0 + 64].rearrange("(k p) n -> p k n", p=P)).then_inc(sem("dtw_in"), 16)
            pool.memset(stat[:, 40:41], -0.5).then_inc(sem("pool_const"), 1)
            pool.wait_ge(sem("pool_const"), 1)

            def power(out, src, waits):
                pool.wait_ge(sem(waits[0]), waits[1])
                pool.tensor_tensor(out, src, stat[:, 40:41], ALU.pow).then_inc(sem("pow_done"), 1)

            def store(dst, src, waits):
                pool.wait_ge(sem(waits[0]), waits[1])
                n_store[0] += 1
                pool.dma_start(dst, src).then_inc(sem("stored"), 16)

            for t in range(NT):
                power(stat[:, t:t + 1], stat[:, 4 + t:5 + t], ("ms_ready", t + 1))
            pool.wait_ge(sem("x_free"), AT["csT"])
            pool.dma_start(scratch.rearrange("d t h l -> h d t l"), csT[0:32]).then_inc(sem("csT_out"), 16)
            pool.wait_ge(sem("csT_out"), 16)

            def load_cs(n):
                g, t = units[n // 2]
                if n >= 4:
                    pool.wait_ge(sem("x_ready"), AT["y"][n // 2 - 2])
                pool.dma_start(ebuf[:, n % 4].rearrange("p h l -> p (h l)"),
                               scratch[n % 2, t, S_HPG * g:S_HPG * (g + 1), :].rearrange("h l -> (h l)")
                               .partition_broadcast(P)).then_inc(sem(f"cs_in{n % 4}"), 16)

            state = t_in["state_ssd"][0, 0]
            new_state = t_out["state"][0, 0]

            def load_h0(g):
                if g:
                    pool.wait_ge(sem("x_ready"), AT["h0"][g - 1])
                for d in range(2):
                    pool.dma_start(h0raw[:, d], state[d, S_HPG * g:S_HPG * (g + 1)].rearrange(
                        "(c a) p n -> (a p) c n", a=2)).then_inc(sem(f"h0_in_d{d}"), 16)

            load_h0(0)
            for n in range(4):
                load_cs(n)
            def y_power(u):
                power(stat[:, 8 + u % 2:9 + u % 2], stat[:, 10 + u % 2:11 + u % 2], ("yms_ready", u + 1))

            for u, (g, t) in enumerate(units):
                if u:
                    y_power(u - 1)
                pool.wait_ge(sem("m_ready"), 2 * u + 2)
                pool.tensor_tensor(ebuf[:, (2 * u) % 4], ebuf[:, (2 * u) % 4], ebuf[:, (2 * u + 1) % 4], ALU.add)\
                    .then_inc(sem("m_sum"), 1)
                if t == 0:
                    if g + 1 < S_GROUPS:
                        load_h0(g + 1)
                    for d in range(2):
                        store(new_state[d, S_HPG * g:S_HPG * (g + 1)].rearrange("(c a) p n -> (a p) c n", a=2),
                              st_out[:, d].rearrange("p (c n) -> p c n", n=P), ("x_free", AT["st"][2 * g + d]))
                if u + 2 < len(units):
                    load_cs(2 * u + 4)
                    load_cs(2 * u + 5)
            y_power(len(units) - 1)
            pool.wait_ge(sem("ssd_over"), 1)
            pool.dma_start(ck_raw, t_in["cache_k"][0, 0].rearrange("s h d -> s (h d)")).then_inc(sem("ck_in"), 16)
            pool.wait_ge(sem("p_ready"), AT["q"] + 1)
            pool.dma_start(vT[:, 1, :], t_in["cache_v"][0, 0].rearrange("s h d -> s (h d)")).then_inc(sem("cv_in"), 16)
            store(t_out["k"][0, 0].rearrange("s h d -> s (h d)"), k_out, ("x_free", AT["kout"][1]))
            store(t_out["v"][0, 0].rearrange("s h d -> s (h d)"), vT[:, 0, :], ("p_free", AT["v"]))
            for i in range(A_HEADS * NT):
                power(stat[:, 12 + i % 4:13 + i % 4], stat[:, 16 + i % 4:17 + i % 4], ("oms_ready", i + 1))
            pool.wait_ge(sem("p_ready"), AT["scores"][-1])
            pool.dma_start(x[:, 0, :], t_in["x_prompt"][0]).then_inc(sem("x_again"), 16)
            pool.dma_start(x[:, 1:3, :], t_in["x_sample"][0].rearrange("(t p) d -> p t d", p=P)).then_inc(sem("x_again"), 16)
            pool.wait_ge(sem("attn_over"), 1)
            pool.dma_start(wr, t_in["w_router"][0].rearrange("(k p) n -> p k n", p=P)).then_inc(sem("wr_in"), 16)
            for t in range(NT):
                power(stat[:, 20 + t:21 + t], stat[:, 24 + t:25 + t], ("ms2_ready", t + 1))
                power(stat[:, t:t + 1], stat[:, 4 + t:5 + t], ("ms3_ready", t + 1))
            pool.wait_ge(sem("x_ready"), AT["dispatched"])
            pool.memset(y, 0.0).then_inc(sem("comb_done"), 1)
            pool.memset(lam_t[:, 4:5], 0.0).then_inc(sem("comb_done"), 1)
            for t in range(NT):
                power(stat[:, 20 + t:21 + t], stat[:, 24 + t:25 + t], ("ms4_ready", t + 1))
            store(t_out["xp"][0], x[:, 0, :], ("out_ready", 1))
            for t in (1, 2):
                store(t_out["xs"][0, (t - 1) * P:t * P, :], x[:, t, :], ("out_ready", t + 1))
            pool.wait_ge(sem("stored"), 16 * n_store[0])

        @block.scalar
        def _(act):
            n_p, n_t, n_c = [0], [0], [0]
            use_of_conv = []

            def p_take():
                n = n_p[0]
                n_p[0] += 1
                act.wait_ge(sem("p_ready"), n + 1)
                return psum[:, n % 4]

            def p_free(ins):
                return ins.then_inc(sem("p_free"), 1)

            def t_write():
                if n_t[0]:
                    act.wait_ge(sem("t_used"), n_t[0])
                n_t[0] += 1

            def rows(dst, at_, src, n, s):
                act.dma_start(dst[at_:at_ + n, :], src.rearrange("(a p) -> a p", p=P)).then_inc(sem(s), 16)

            rows(rows_a, 80, t_in["c_ctx"], 8, "rows_a_in")
            rows(rows_a, 88, t_in["c"][0], 8, "rows_a_in")
            rows(rows_a, 0, t_in["b_ada"][0], 48, "rows_a_in")
            for i, name in enumerate(("g_pre_mix", "g_post_mix", "g_pre_ffn", "g_post_ffn")):
                rows(rows_a, 48 + 8 * i, t_in[name][0], 8, "rows_a_in")
            act.dma_start(x0[:, 0, :], t_in["x_prompt"][0]).then_inc(sem("x_in"), 16)
            act.dma_start(x0[:, 1:3, :], t_in["x_sample"][0].rearrange("(t p) d -> p t d", p=P)).then_inc(sem("x_in"), 16)
            rows(rows_b, 0, t_in["conv_w"][0].rearrange("k c -> (k c)"), 72, "rows_b_in")
            rows(rows_b, 72, t_in["conv_b"][0], 24, "rows_b_in")
            rows(rows_b, 96, t_in["w_ssd_norm"][0], 16, "rows_b_in")
            rows(rows_b, 112, t_in["w_subln"][0], 1, "rows_b_in")
            act.wait_ge(sem("x_free"), 1)
            act.activation(junk1[:, 0:16], vec_a[:, 80:96], ACT.Tanh, scale=0.5).then_inc(sem("cond_t"), 1)
            act.wait_ge(sem("x_in"), 32)
            for t in range(NT):
                if t:
                    act.wait_ge(sem("sq_ready"), t)
                act.activation(junk0, x0[:, t, :], ACT.Square, accum_out=stat[:, 32 + t:33 + t]).then_inc(sem("sq_ready"), 1)

            def ada(j):
                b = p_take()
                if j >= 2:
                    act.wait_ge(sem("x_ready"), AT["ada_x"][j - 2])
                p_free(act.activation(mod_rows[:, j % 2, :], b[:, :], ACT.Copy))

            for j in range(4):
                ada(j)

            def conv_in(i, ch):
                b = p_take()
                r, cc = raw2[:, i % 2], conv2[:, i % 2]
                if i >= 2:
                    act.wait_ge(sem("t_used"), use_of_conv[i - 2])
                act.activation(r[:, 1:P + 1], b[:, 0:P], ACT.Copy)
                p_free(act.activation(r[:, P + 2:PAD + 1], b[:, P:NTOK], ACT.Copy))
                act.wait_ge(sem("p_free"), n_p[0])
                act.activation(cc, r[:, 1:PAD + 1], ACT.Identity, scale=vec_b[:, 24 + ch:25 + ch],
                               bias=vec_b[:, 72 + ch:73 + ch]).then_inc(sem("conv_in"), 1)

            def conv_tanh(i):
                act.wait_ge(sem("conv_mid"), i + 1)
                t_write()
                use_of_conv.append(n_t[0])
                act.activation(th[:, 0:PAD], conv2[:, i % 2], ACT.Tanh).then_inc(sem("t_ready"), 1)

            def z_in(g, t):
                b = p_take()
                p_free(act.activation(zs2[:, g % 2, t, :], b[:, :], ACT.Copy, scale=0.5))
                return n_p[0]

            def z_tanh(g, t, n):
                act.wait_ge(sem("p_free"), n)
                t_write()
                act.activation(th, zs2[:, g % 2, t, :], ACT.Tanh).then_inc(sem("t_ready"), 1)

            def items(todo):
                prev = None
                for it in [*todo, None]:
                    if it and it[0] == "x":
                        i = n_c[0]
                        n_c[0] += 1
                        conv_in(i, 4 * it[1] + it[2])
                        nxt = (conv_tanh, i)
                    elif it and it[0] == "z":
                        nxt = (z_tanh, it[1], it[2], z_in(it[1], it[2]))
                    elif it:
                        b = p_take()
                        p_free(act.activation(gsT[:, it[1], :], b[:, 0:NTOK], ACT.Tanh, scale=0.5))
                        nxt = None
                    else:
                        nxt = None
                    if prev:
                        prev[0](*prev[1:])
                    prev = nxt

            act.wait_ge(sem("pads_ready"), 1)
            act.wait_ge(sem("x_free"), 2)
            items([("x", 4 + j, c_) for j in range(2) for c_ in range(4)])
            act.wait_ge(sem("dtp_in"), 48)
            for lo, n in ((0, 1), (1, 2)):
                b = p_take()
                p_free(act.activation(dt[:, lo:lo + n, :], b[:, 0:64 * n].rearrange("p (t h) -> p t h", h=64), ACT.Copy))
            act.wait_ge(sem("dt_abs"), 1)
            act.activation(t_tot, tmp_a, ACT.Exp).then_inc(sem("dt_exp"), 1)
            act.activation(a_neg, a_neg, ACT.Exp).then_inc(sem("a_exp"), 1)
            act.wait_ge(sem("dt_one"), 1)
            act.activation(e_cs, cs, ACT.Ln).then_inc(sem("dt_log"), 1)
            items([("x", 0, c_) for c_ in range(4)] + [("z", 0, t) for t in range(NT)])
            act.wait_ge(sem("cs_ready"), 1)
            act.activation(e_cs, cs, ACT.Exp).then_inc(sem("exp_small"), 1)
            act.activation(e_tot, t_tot, ACT.Exp).then_inc(sem("exp_small"), 1)
            act.activation(dec_dt, tmp_a, ACT.Exp).then_inc(sem("exp_small"), 1)
            act.wait_ge(sem("lam_dot"), 1)
            act.activation(lam_t[:, 2:4], lam_t[:, 0:2], ACT.Exp).then_inc(sem("lam_exp"), 1)

            for u, (g, t) in enumerate(units):
                for d in range(2):
                    n = 2 * u + d
                    act.wait_ge(sem("d_ready"), n + 1)
                    e_ = ebuf[:, n % 4].rearrange("p h l -> p (h l)")
                    act.activation(e_, e_, ACT.Exp).then_inc(sem("e_ready"), 1)
                items(beside(g, t))
                act.wait_ge(sem("y_ready"), u + 1)
                act.activation(junk, y1[:, u % 2, :], ACT.Square, accum_out=stat[:, 36 + u % 2:37 + u % 2]).then_inc(sem("ysq_ready"), 1)

            for i in range(KT):
                b = p_take()
                if i >= 2:
                    act.wait_ge(sem("merged_ready"), i - 1)
                else:
                    act.wait_ge(sem("ssd_over"), 1)
                p_free(act.activation(proj_tmp[:, i % 2, :], b[:, 0:NTOK], ACT.Copy, scale=0.5))
            for i in range(2 * A_HEADS):
                b = p_take()
                h = i % A_HEADS
                if i == 0:
                    act.wait_ge(sem("merged_ready"), KT)
                if i >= 2:
                    act.wait_ge(sem("rope_done"), i - 1)
                dst = qT[:, h, 0:P] if i < A_HEADS else kT[:, h, 0:P]
                act.activation(dst, b[:, 0:P], ACT.Copy)
                p_free(act.activation(rope_raw[:, i % 2, :], b[:, P:NTOK], ACT.Copy))
            for j in range(2):
                for t in range(NT):
                    b = p_take()
                    vb = 0 if t == 0 else t + 1
                    p_free(act.activation(vT[:, vb, j * CW:(j + 1) * CW], b[:, :], ACT.Copy))
            def exps(i):
                kn = P if i % NT == 0 else NTOK
                act.wait_ge(sem("nmax_ready"), i + 1)
                if i >= 2:
                    act.wait_ge(sem("a_ready"), i - 1)
                for m in range(2):
                    b = p_take()
                    p_free(act.activation(prob[:, i % 2, m, 0:kn], b[:, 0:kn], ACT.Exp, scale=A_HD ** -0.5,
                                          bias=neg_max[:, i % 2, m:m + 1], accum_out=row_sum[:, i % 2, m:m + 1]))

            exps(0)
            for i in range(A_HEADS * NT):
                if i + 1 < A_HEADS * NT:
                    exps(i + 1)
                for kind, n in beside_attn.get(i, []):
                    if kind == "ga":
                        b = p_take()
                        p_free(act.activation(gaT[:, n, :], b[:, 0:NTOK], ACT.Tanh, scale=0.5))
                    else:
                        ada(n)
            for i in range(KT):
                b = p_take()
                if i >= 2:
                    act.wait_ge(sem("merged_ready"), KT + i - 1)
                p_free(act.activation(proj_tmp[:, i % 2, :], b[:, 0:NTOK], ACT.Copy, scale=0.5))
            act.wait_ge(sem("x_free"), AT["oTa"])
            for t in range(NT):
                for j in range(2):
                    b = p_take()
                    p_free(act.activation(y[:, t, j * CW:(j + 1) * CW], b[:, :], ACT.Copy))
                act.wait_ge(sem("p_free"), n_p[0])
                if t == 0:
                    act.wait_ge(sem("attn_over"), 1)
                act.activation(xn[:, t, :], y[:, t, :], ACT.Square, accum_out=stat[:, 32 + t:33 + t]).then_inc(sem("sq_ready"), 1)
                act.wait_ge(sem("xnew_ready"), t + 1)
                act.activation(xn[:, t, :], x[:, t, :], ACT.Square, accum_out=stat[:, 32 + t:33 + t]).then_inc(sem("sq_ready"), 1)
            act.wait_ge(sem("lgm_ready"), 1)
            act.activation(lg, lg, ACT.Exp).then_inc(sem("lge_ready"), 1)
            def diagonals(n):
                cnd, j = n // 2, n % 2
                for q in range(4):
                    act.activation(diag[:, n % 2, q, :], ident, ACT.Copy,
                                   scale=gpost[:, KT + 4 * j + q, cnd:cnd + 1]).then_inc(sem("diag2_ready"), 1)
            diagonals(0)
            diagonals(1)
            n0 = n_p[0]
            for n in range(4):
                b = p_take()
                p_free(act.activation(Gb[:, n // 2, (n % 2) * CW:(n % 2 + 1) * CW], b[:, :], ACT.Copy))
                if n < 2:
                    diagonals(n + 2)
            for j in range(2):
                act.activation(route[:, 4 + j:5 + j], stat[:, 32 + j:33 + j], ACT.Copy).then_inc(sem(f"d_free{j}"), 1)
            with act.Fori(0, NE // GE) as g:
                for i in range(GE):
                    for j in range(4):
                        act.wait_ge(sem("gu_ready"), g * 16 + (4 * i + j + 1))
                        act.wait_ge(sem("h_done"), g * 16 + (4 * i + j + 1))
                        act.activation(sg[:, j % 2, :], psum[:, j % 2, 0:2 * P], ACT.Silu).then_inc(sem("sg_ready"), 1)
                    for j in range(2):
                        act.wait_ge(sem(f"d_ready{j}"), g * GE + (i + 1))
                        for q in range(2):
                            c0 = j * CW + q * 2 * P
                            for dst, lo in ((stage_s, 0), (stage_p, CAP_S)):
                                cp = act.activation(dst[CAP_S * i:CAP_S * (i + 1), c0:c0 + 2 * P],
                                                    psum[HALF * q + lo:HALF * q + lo + CAP_S, 5 + j, 0:2 * P], ACT.Copy)
                        cp.then_inc(sem(f"d_free{j}"), 1)
            for t in range(NT):
                act.wait_ge(sem("comb_done"), 6 * (NE // GE - 1) + 2 * (t + 2))
                if t:
                    act.wait_ge(sem("sq_ready"), 9 + t)
                act.activation(last_junk, y[:, t, :], ACT.Square,
                               accum_out=stat[:, 32 + t:33 + t]).then_inc(sem("sq_ready"), 1)

        @block.vector
        def _(dve):
            c = Count(dve, sem("dve_step"))
            n_x, n_t, n_c = [0], [0], [0]
            z_at = {}

            def x_take():
                n = n_x[0]
                n_x[0] += 1
                dve.wait_ge(sem("x_ready"), n + 1)
                return psum[:, 4 + n % 4]

            def x_free(ins):
                return ins.then_inc(sem("x_free"), 1)

            def link(ins):
                c.do(ins)
                c.settle()

            def x_settle():
                dve.wait_ge(sem("x_free"), n_x[0])

            def wide(v, n):
                return v.unsqueeze(2).broadcast_to([v.shape[0], v.shape[1], n])

            b = x_take()
            x_free(dve.tensor_copy(vec_a, b[:, 0:96]))
            b = x_take()
            dve.tensor_scalar(vec_b[:, 0:96], b[:, 0:96], 0.5, None, ALU.mult)
            dve.tensor_scalar(vec_b[:, 112:113], b[:, 112:113], 1.0 - LAM_INIT, None, ALU.mult)
            x_free(dve.tensor_copy(vec_b[:, 96:112], b[:, 96:112]))
            x_settle()
            dve.wait_ge(sem("cond_t"), 1)
            dve.memset(cond[:, :, 2:32], 0.0)
            link(dve.tensor_scalar(junk1[:, 16:32], vec_a[:, 80:96], 0.5, None, ALU.mult))
            dve.scalar_tensor_tensor(cond[:, :, 0:2].rearrange("p k c -> p c k"), junk1[:, 0:16].rearrange("p (c k) -> p c k", c=2),
                                     1.0, junk1[:, 16:32].rearrange("p (c k) -> p c k", c=2), ALU.add, ALU.mult)\
               .then_inc(sem("cond_ready"), 1)

            def normalise(out_of, src_of, m, r, signal, done, sq):
                for t in range(NT):
                    dve.wait_ge(sem("sq_ready"), sq + t + 1)
                    dve.tensor_scalar(stat[:, m + t:m + t + 1], stat[:, 32 + t:33 + t], 1.0 / D, EPS, ALU.mult, ALU.add)\
                       .then_inc(sem(signal), 1)
                for t in range(NT):
                    dve.wait_ge(sem("pow_done"), pw[0] + t + 1)
                    dve.tensor_scalar(out_of(t), src_of(t), stat[:, r + t:r + t + 1], None, ALU.mult)\
                       .then_inc(sem(done), 1)
                pw[0] += NT

            pw = [0]
            normalise(lambda t: x0[:, t, :], lambda t: x0[:, t, :], 4, 0, "ms_ready", "xn_ready", 0)

            dve.wait_ge(sem("lam_in"), 64)
            link(dve.tensor_tensor(lam_in[:, 0:4:2, :], lam_in[:, 0:4:2, :], lam_in[:, 1:4:2, :], ALU.mult))
            dve.tensor_reduce(lam_t[:, 0:2], lam_in[:, 0:4:2, :], AX.X, ALU.add).then_inc(sem("lam_dot"), 1)

            def ada_cm(j):
                b = x_take()
                x_free(dve.tensor_tensor(mod[:, 4 * j:4 * j + 4, :], b[:, 0:8].rearrange("p (a c) -> p a c", c=2),
                                         wide(vec_a[:, 4 * j:4 * j + 4], 2), ALU.add))

            def affine(dst, sc, sh, gain):
                dve.scalar_tensor_tensor(dst[:, 0:KT, :], mod[:, sc:sc + KT, :], 1.0, wide(vec_a[:, gain:gain + KT], 2),
                                         ALU.add, ALU.mult)
                link(dve.tensor_copy(dst[:, KT:2 * KT, :], mod[:, sh:sh + KT, :]))

            for j in range(4):
                ada_cm(j)
            x_settle()
            affine(aff1, 8, 0, 48)
            dve.memset(lam_t[:, 7:8], 0.0)

            def to_cm(dst, aff):
                for k in range(KT):
                    b = x_take()
                    dve.tensor_scalar(dst[:, k, 0:P], b[:, 0:P], aff[:, k, 0:1], aff[:, KT + k, 0:1], ALU.mult, ALU.add)
                    x_free(dve.tensor_scalar(dst[:, k, P:NTOK], b[:, P:NTOK], aff[:, k, 1:2], aff[:, KT + k, 1:2],
                                             ALU.mult, ALU.add))

            to_cm(h1T, aff1)
            dve.wait_ge(sem("x_ready"), n_x[0])
            for col in (0, P + 1, PAD + 1):
                last = dve.memset(raw2[:, :, col:col + 1], 0.0)
            last.then_inc(sem("pads_ready"), 1)

            def conv_mid(i, ch):
                dve.wait_ge(sem("conv_in"), i + 1)
                r, cc = raw2[:, i % 2], conv2[:, i % 2]
                link(dve.scalar_tensor_tensor(cc, r[:, 0:PAD], vec_b[:, ch:ch + 1], cc, ALU.mult, ALU.add))
                dve.scalar_tensor_tensor(cc, r[:, 2:PAD + 2], vec_b[:, 48 + ch:49 + ch], cc, ALU.mult, ALU.add)\
                   .then_inc(sem("conv_mid"), 1)

            def conv_out(i, dst):
                dve.wait_ge(sem("t_ready"), n_t[0] + 1)
                n_t[0] += 1
                dve.scalar_tensor_tensor(dst, th[:, 0:PAD], 1.0, conv2[:, i % 2], ALU.add, ALU.mult)\
                   .then_inc(sem("t_used"), 1)

            def z_out(g, t):
                dve.wait_ge(sem("t_ready"), n_t[0] + 1)
                n_t[0] += 1
                z_ = zs2[:, g % 2, t, :]
                dve.scalar_tensor_tensor(z_, th, 1.0, z_, ALU.add, ALU.mult).then_inc(sem("t_used"), 1)
                z_at[g, t] = n_t[0]

            def items(todo):
                prev = None
                for it in [*todo, None]:
                    nxt = None
                    if it and it[0] == "x":
                        i = n_c[0]
                        n_c[0] += 1
                        conv_mid(i, 4 * it[1] + it[2])
                        nxt = (conv_out, i, BC[:, 4 * (it[1] - 4) + it[2], :] if it[1] >= 4 else xs[:, it[2], :])
                    elif it and it[0] == "z":
                        nxt = (z_out, it[1], it[2])
                    if prev:
                        prev[0](*prev[1:])
                    prev = nxt

            items([("x", 4 + j, c_) for j in range(2) for c_ in range(4)])
            dve.wait_ge(sem("p_free"), AT["dt"])
            dve.wait_ge(sem("dtp_in"), 48)
            bias3 = dt_bias.unsqueeze(1).broadcast_to([P, NT, 64])
            link(dve.tensor_tensor(dt, dt, bias3, ALU.add))
            link(dve.tensor_scalar(cs, dt, -1.0, None, ALU.mult))
            dve.tensor_tensor(tmp_a, dt, cs, ALU.min).then_inc(sem("dt_abs"), 1)
            dve.wait_ge(sem("dt_exp"), 1)
            dve.tensor_scalar(cs, t_tot, 1.0, None, ALU.add).then_inc(sem("dt_one"), 1)
            dve.wait_ge(sem("dt_one"), 1)
            link(dve.tensor_scalar(tmp_a, cs, 1.0, None, ALU.subtract))
            link(dve.tensor_scalar(dec_dt, tmp_a, 0.0, None, ALU.is_equal))
            link(dve.tensor_tensor(tmp_a, tmp_a, dec_dt, ALU.add))
            link(dve.reciprocal(tmp_a, tmp_a))
            link(dve.tensor_tensor(tmp_a, tmp_a, t_tot, ALU.mult))
            dve.wait_ge(sem("dt_log"), 1)
            link(dve.tensor_tensor(e_cs, e_cs, dec_dt, ALU.add))
            link(dve.tensor_tensor(e_cs, e_cs, tmp_a, ALU.mult))
            link(dve.scalar_tensor_tensor(dt, dt, 0.0, e_cs, ALU.max, ALU.add))
            dve.wait_ge(sem("a_exp"), 1)
            link(dve.tensor_scalar(a_neg, a_neg, -1.0, None, ALU.mult))
            dve.tensor_tensor(tmp_a, dt, a_neg.unsqueeze(1).broadcast_to([P, NT, 64]), ALU.mult).then_inc(sem("da_ready"), 1)
            items([("x", 0, c_) for c_ in range(4)] + [("z", 0, t) for t in range(NT)])
            for t in range(NT):
                b = x_take()
                x_free(dve.tensor_copy(BTM[:, t, :], b[:, :]))
            b = x_take()
            x_free(dve.tensor_copy(cs, b[:, 0:NT * 64].rearrange("p (t h) -> p t h", h=64)))
            b = x_take()
            x_free(dve.tensor_copy(t_tot, b[:, 0:NT * 64].rearrange("p (t h) -> p t h", h=64)))
            x_settle()
            for d in range(2):
                b = x_take()
                x_free(dve.tensor_copy(csT[0:32, d], b[0:32, 0:NTOK].rearrange("p (t l) -> p t l", l=P)))
            dve.wait_ge(sem("x_ready"), n_x[0])
            dve.tensor_tensor(tmp_a, t_tot, cs, ALU.subtract).then_inc(sem("cs_ready"), 1)
            dve.wait_ge(sem("exp_small"), 3)
            link(dve.tensor_tensor(dec_dt, dec_dt, dt, ALU.mult))
            dve.wait_ge(sem("lam_exp"), 1)
            link(dve.tensor_tensor(lam_t[:, 4:5], lam_t[:, 3:4], lam_t[:, 2:3], ALU.subtract))
            link(dve.tensor_scalar(lam_t[:, 4:5], lam_t[:, 4:5], LAM_INIT, None, ALU.subtract))

            def decayed(d, t, g):
                dve.tensor_tensor(xdec[:, d].rearrange("p (h e) -> p h e", e=S_HD),
                                  xTM[:, t].rearrange("p (h e) -> p h e", e=S_HD),
                                  wide(dec_dt[:, t, 32 * d + 8 * g:32 * d + 8 * g + 8], S_HD), ALU.mult)\
                   .then_inc(sem("xdec_ready"), 1)

            def mean_square(u):
                dve.wait_ge(sem("ysq_ready"), u + 1)
                dve.tensor_scalar(stat[:, 10 + u % 2:11 + u % 2], stat[:, 36 + u % 2:37 + u % 2], 1.0 / 512, EPS,
                                  ALU.mult, ALU.add).then_inc(sem("yms_ready"), 1)

            def rstd_of(u):
                dve.wait_ge(sem("pow_done"), pw[0] + 1)
                pw[0] += 1
                dve.tensor_scalar(y1[:, u % 2, :], y1[:, u % 2, :], stat[:, 8 + u % 2:9 + u % 2], None, ALU.mult)\
                   .then_inc(sem("yn_ready"), 1)

            def o_out(u):
                g, t = units[u]
                b = x_take()
                for c_ in range(4):
                    last = dve.tensor_scalar(oT[:, 4 * g + c_, t * P:(t + 1) * P], b[:, c_ * P:(c_ + 1) * P],
                                             vec_b[:, 96 + 4 * g + c_:97 + 4 * g + c_], None, ALU.mult)
                x_free(last)

            dve.wait_ge(sem("csT_out"), 16)
            for u, (g, t) in enumerate(units):
                hd = slice(S_HPG * g, S_HPG * (g + 1))
                if u:
                    mean_square(u - 1)
                if t == 0:
                    for tt in range(NT):
                        b = x_take()
                        x_free(dve.tensor_copy(xTM[:, tt, :], b[:, :]))
                    for d in range(2):
                        b = x_take()
                        x_free(dve.tensor_copy(h0T[:, d, :], b[:, :]))
                    x_settle()
                b = x_take()
                for d, tri in ((0, tri_f), (1, tri_b)):
                    last = dve.tensor_tensor(cbm[:, u % 2, d, :], b[:, 0:P], tri, ALU.mult)
                x_free(last)
                if t < 2:
                    if t == 1:
                        dve.wait_ge(sem("x_ready"), n_x[0])
                    decayed(0, t, g)
                    decayed(1, 2 * t, g)
                for d in range(2):
                    n = 2 * u + d
                    dve.wait_ge(sem(f"cs_in{n % 4}"), 16 * (n // 4 + 1))
                    for h in range(S_HPG):
                        e_ = ebuf[:, n % 4, h, :]
                        last = dve.tensor_scalar(e_, e_, cs[:, t, 32 * d + 8 * g + h:32 * d + 8 * g + h + 1], 0.0,
                                                 ALU.subtract, ALU.min)
                    last.then_inc(sem("d_ready"), 1)
                if u:
                    rstd_of(u - 1)
                x_settle()
                for d in range(2):
                    n = 2 * u + d
                    dve.wait_ge(sem("e_ready"), n + 1)
                    for h in range(S_HPG):
                        e_ = ebuf[:, n % 4, h, :]
                        last = dve.scalar_tensor_tensor(e_, e_, dt[:, t, 32 * d + 8 * g + h:32 * d + 8 * g + h + 1],
                                                        cbm[:, u % 2, d, :], ALU.mult, ALU.mult)
                    last.then_inc(sem("m_ready"), 1)
                if t == 0:
                    for d in range(2):
                        b = x_take()
                        if g:
                            dve.wait_ge(sem("stored"), 32 * g)
                        x_free(dve.tensor_copy(st_out[:, d, :], b[:, :]))
                if t == 1:
                    for d in range(2):
                        b = x_take()
                        tt = 1 + d
                        link(dve.tensor_tensor(hT1[:, d].rearrange("p (h e) -> p h e", e=S_HD),
                                               h0T[:, d].rearrange("p (h e) -> p h e", e=S_HD),
                                               wide(e_tot[:, tt, 32 * d + 8 * g:32 * d + 8 * g + 8], S_HD), ALU.mult))
                        x_free(dve.tensor_tensor(hT1[:, d], hT1[:, d], b[:, :], ALU.add))
                items(beside(g, t))
                if u:
                    o_out(u - 1)
                yv = y1[:, u % 2, :]
                yh = yv.rearrange("p (h e) -> p h e", e=S_HD)
                link(dve.tensor_tensor(yh, xTM[:, t].rearrange("p (h e) -> p h e", e=S_HD), wide(d_skip[:, hd], S_HD), ALU.mult))
                b = x_take()
                x_free(dve.tensor_tensor(yv, yv, b[:, :], ALU.add))
                x_settle()
                if t:
                    for d in range(2):
                        b = x_take()
                        x_free(dve.tensor_tensor(ytmp.rearrange("p (h e) -> p h e", e=S_HD),
                                                 b[:, :].rearrange("p (h e) -> p h e", e=S_HD),
                                                 wide(e_cs[:, t, 32 * d + 8 * g:32 * d + 8 * g + 8], S_HD), ALU.mult))
                        x_settle()
                        link(dve.tensor_tensor(yv, yv, ytmp, ALU.add))
                dve.wait_ge(sem("t_used"), z_at[g, t])
                dve.tensor_tensor(yv, yv, zs2[:, g % 2, t, :], ALU.mult).then_inc(sem("y_ready"), 1)
            mean_square(len(units) - 1)
            rstd_of(len(units) - 1)
            o_out(len(units) - 1)
            dve.wait_ge(sem("stored"), 32 * S_GROUPS)
            dve.wait_ge(sem("p_free"), AT["gs"])
            x_settle()
            dve.memset(lam_t[:, 6:7], 0.0).then_inc(sem("ssd_over"), 1)
            for i in range(KT):
                dve.wait_ge(sem("p_free"), AT["gs"] + i + 1)
                dve.scalar_tensor_tensor(mergedT[:, i, :], gsT[:, i, :], 1.0, proj_tmp[:, i % 2, :],
                                         ALU.add, ALU.mult).then_inc(sem("merged_ready"), 1)
            for i in range(2 * A_HEADS):
                h = i % A_HEADS
                b = x_take()
                dst = qT[:, h, P:NTOK] if i < A_HEADS else kT[:, h, 2 * P:4 * P]
                c.do(dve.tensor_tensor(dst, rope_raw[:, i % 2, :], cos_t, ALU.mult))
                x_free(dve.tensor_tensor(rope_tmp, b[:, 0:2 * P], sin_t, ALU.mult))
                c.settle()
                x_settle()
                dve.tensor_tensor(dst, dst, rope_tmp, ALU.add).then_inc(sem("rope_done"), 1)
                dve.wait_ge(sem("rope_done"), i + 1)
            for j in range(2):
                b = x_take()
                x_free(dve.tensor_copy(kT[:, 4 * j:4 * j + 4, P:2 * P], b[:, :].rearrange("p (h s) -> p h s", s=P)))
            for j in range(2):
                b = x_take()
                x_free(dve.tensor_copy(k_out[:, j * 512:(j + 1) * 512], b[:, :]))

            NA = A_HEADS * NT
            keys = lambda i: P if i % NT == 0 else NTOK
            late = []
            for i in range(NA + 5):
                if i < NA:
                    n = AT["scores"][i]
                    dve.wait_ge(sem("p_ready"), n + 2)
                    b0 = n % 4
                    link(dve.tensor_reduce(row_max[:, i % 2, :], psum[:, b0:b0 + 2, 0:keys(i)], AX.X, ALU.max))
                    dve.tensor_scalar(neg_max[:, i % 2, :], row_max[:, i % 2, :], -(A_HD ** -0.5), None, ALU.mult)\
                       .then_inc(sem("nmax_ready"), 1)
                if 4 <= i <= NA + 3:
                    j = i - 4
                    dve.wait_ge(sem("pow_done"), pw[0] + 1)
                    pw[0] += 1
                    dve.tensor_scalar(o_sb[:, j % 4, :], o_sb[:, j % 4, :], stat[:, 12 + j % 4:13 + j % 4], None, ALU.mult)\
                       .then_inc(sem("on_ready"), 1)
                if 1 <= i <= NA:
                    j = i - 1
                    n = keys(j)
                    dve.wait_ge(sem("p_free"), AT["scores"][j] + 2)
                    link(dve.reciprocal(inv_sum[:, j % 2, :], row_sum[:, j % 2, :]))
                    c.do(dve.tensor_tensor(inv_sum[:, j % 2, 1:2], inv_sum[:, j % 2, 1:2], lam_t[:, 4:5], ALU.mult))
                    link(dve.tensor_scalar(amix[:, j % 2, 0:n], prob[:, j % 2, 0, 0:n], inv_sum[:, j % 2, 0:1], None, ALU.mult))
                    dve.scalar_tensor_tensor(amix[:, j % 2, 0:n], prob[:, j % 2, 1, 0:n], inv_sum[:, j % 2, 1:2],
                                             amix[:, j % 2, 0:n], ALU.mult, ALU.add).then_inc(sem("a_ready"), 1)
                for j in late:
                    ada_cm(j)
                late = [n for kind, n in beside_attn.get(i, []) if kind == "ada"]
                if 2 <= i <= NA + 1:
                    j = i - 2
                    b = x_take()
                    x_free(dve.tensor_copy(aT[:, j % 2, 0:keys(j)], b[:, 0:keys(j)]))
                if 3 <= i <= NA + 2:
                    j = i - 3
                    b = x_take()
                    x_free(dve.tensor_copy(o_sb[:, j % 4, :], b[:, 0:P]))
                    x_settle()
                    if j:
                        dve.wait_ge(sem("oms_ready"), j)
                    dve.tensor_tensor_reduce(out=o_junk, in0=o_sb[:, j % 4, :], in1=o_sb[:, j % 4, :],
                                             scale=1.0 / A_VD, scalar=EPS, op0=ALU.mult, op1=ALU.add,
                                             accum_out=stat[:, 16 + j % 4:17 + j % 4]).then_inc(sem("oms_ready"), 1)
                if i >= 5:
                    j = i - 5
                    h, t = divmod(j, NT)
                    b = x_take()
                    x_free(dve.tensor_scalar(oTa[:, h, t * P:(t + 1) * P], b[:, 0:P], vec_b[:, 112:113], None, ALU.mult))
            x_settle()
            affine(aff2, 32, 24, 64)
            dve.tensor_tensor(gpost[:, 0:KT, :], mod[:, 16:24, :], wide(vec_a[:, 56:64], 2), ALU.mult)
            link(dve.tensor_tensor(gpost[:, KT:2 * KT, :], mod[:, 40:48, :], wide(vec_a[:, 72:80], 2), ALU.mult))
            for i in range(KT):
                dve.wait_ge(sem("p_free"), AT["attn_end"] + i + 1)
                tv = proj_tmp[:, i % 2, :]
                link(dve.scalar_tensor_tensor(tv, gaT[:, i, :], 1.0, tv, ALU.add, ALU.mult))
                dve.tensor_tensor(mergedT[:, i, :], mergedT[:, i, :], tv, ALU.add).then_inc(sem("merged_ready"), 1)

            def spread():
                def diagonals(n):
                    for q in range(4):
                        dve.tensor_scalar(diag[:, n % 2, q, :], ident, gpost[:, 4 * (n % 2) + q, n // 2:n // 2 + 1],
                                          None, ALU.mult).then_inc(sem("diag_ready"), 1)
                diagonals(0)
                diagonals(1)
                for n in range(4):
                    b = x_take()
                    x_free(dve.tensor_copy(Gb[:, n // 2, (n % 2) * CW:(n % 2 + 1) * CW], b[:, :]))
                    if n < 2:
                        diagonals(n + 2)
                x_settle()
            dve.wait_ge(sem("merged_ready"), 2 * KT)
            dve.wait_ge(sem("stored"), 32 * S_GROUPS + 32)
            spread()
            dve.memset(lam_t[:, 6:7], 0.0).then_inc(sem("attn_over"), 1)

            def residual(m, r, signal, done, sq):
                for t in range(NT):
                    dve.wait_ge(sem("sq_ready"), sq + t + 1)
                    dve.tensor_scalar(stat[:, m + t:m + t + 1], stat[:, 32 + t:33 + t], 1.0 / D, EPS, ALU.mult, ALU.add)\
                       .then_inc(sem(signal), 1)
                for t in range(NT):
                    dve.wait_ge(sem("pow_done"), pw[0] + t + 1)
                    link(dve.scalar_tensor_tensor(y[:, t, :], y[:, t, :], stat[:, r + t:r + t + 1],
                                                  Gb[:, min(t, 1), :], ALU.mult, ALU.mult))
                    dve.tensor_tensor(x[:, t, :], x[:, t, :], y[:, t, :], ALU.add).then_inc(sem(done), 1)
                pw[0] += NT

            dve.wait_ge(sem("x_again"), 32)
            def mean_square(dst, src, n, signal):
                dve.wait_ge(sem("sq_ready"), n)
                dve.tensor_scalar(dst, src, 1.0 / D, EPS, ALU.mult, ALU.add).then_inc(sem(signal), 1)

            def tile_norm(t):
                s0 = stat[:, 32 + t:33 + t]
                mean_square(stat[:, 24 + t:25 + t], s0, 3 + 2 * t + 1, "ms2_ready")
                dve.wait_ge(sem("pow_done"), pw[0] + 1)
                link(dve.scalar_tensor_tensor(y[:, t, :], y[:, t, :], stat[:, 20 + t:21 + t],
                                              Gb[:, min(t, 1), :], ALU.mult, ALU.mult))
                dve.tensor_tensor(x[:, t, :], x[:, t, :], y[:, t, :], ALU.add).then_inc(sem("xnew_ready"), 1)
                mean_square(stat[:, 4 + t:5 + t], s0, 3 + 2 * t + 2, "ms3_ready")
                dve.wait_ge(sem("pow_done"), pw[0] + 2)
                dve.tensor_scalar(xn[:, t, :], x[:, t, :], stat[:, t:t + 1], None, ALU.mult).then_inc(sem("xn2_ready"), 1)
                pw[0] += 2

            def tile_to_h2(t):
                cnd = min(t, 1)
                for j in range(2):
                    b = x_take()
                    for k in range(4 * j, 4 * j + 4):
                        last = dve.tensor_scalar(h2T[:, k, t * P:(t + 1) * P], b[:, (k - 4 * j) * P:(k - 4 * j + 1) * P],
                                                 aff2[:, k, cnd:cnd + 1], aff2[:, KT + k, cnd:cnd + 1], ALU.mult, ALU.add)
                    x_free(last)

            def logits(t):
                b = x_take()
                x_free(dve.tensor_copy(lg[:, t, :], b[:, 0:NE]))

            tile_norm(0)
            tile_to_h2(0)
            tile_norm(1)
            logits(0)
            tile_to_h2(1)
            tile_norm(2)
            logits(1)
            tile_to_h2(2)
            logits(2)
            x_settle()
            link(dve.tensor_reduce(route[:, 0:NT], lg, AX.X, ALU.max))
            dve.tensor_tensor(lg, lg, wide(route[:, 0:NT], NE), ALU.subtract).then_inc(sem("lgm_ready"), 1)
            dve.wait_ge(sem("lge_ready"), 1)
            link(dve.tensor_reduce(route[:, 0:NT], lg, AX.X, ALU.add))
            link(dve.reciprocal(route[:, 0:NT], route[:, 0:NT]))
            dve.tensor_tensor(affin, lg, wide(route[:, 0:NT], NE), ALU.mult).then_inc(sem("affin_ready"), 1)
            b = x_take()
            x_free(dve.tensor_copy(affT[0:NE, :], b[0:NE, 0:NTOK]))
            x_settle()
            for lo, n, cap, o in ((0, P, CAP_P, 0), (P, 2 * P, CAP_S, CAP_P)):
                for r in range(cap // 8):
                    a_ = affT[0:NE, lo:lo + n]
                    m8 = mx8[0:NE, o + 8 * r:o + 8 * r + 8]
                    link(dve.max(m8, a_))
                    c.do(dve.max_index(idx_u[0:NE, o + 8 * r:o + 8 * r + 8], m8, a_))
                    c.settle()
                    link(dve.match_replace(a_, m8, a_, -1.0))
                link(dve.tensor_copy(idx_f[0:NE, o:o + cap], idx_u[0:NE, o:o + cap]))
            c.do(dve.memset(SG_p[:, :, CAP_P:CAP_S], 0.0))
            c.do(dve.memset(xe[:, :, CAP:HALF], 0.0))
            dve.memset(lam_t[:, 5:6], 0.0).then_inc(sem("h_done"), 1)
            dve.memset(lam_t[:, 6:7], 0.0).then_inc(sem("h_done"), 1)
            dve.memset(lam_t[:, 7:8], 0.0).then_inc(sem("hT_done"), 1)
            for i, (cap, o) in enumerate(((CAP_P, 0), (CAP_S, CAP_P))):
                n = NE * cap
                iv = idx_f[0:NE, o:o + cap].unsqueeze(1).broadcast_to([NE, NE, cap])
                if i:
                    dve.wait_ge(sem("x_ready"), n_x[0])
                dve.tensor_tensor(idx_blk[0:NE, 0:n].rearrange("p (e c) -> p e c", c=cap), iv,
                                  wide(ident[0:NE, 0:NE], cap), ALU.mult).then_inc(sem("idx_ready"), 1)
                b = x_take()
                for tt in range(1 + i):
                    dst = S_s[:, tt, :] if i else S_p
                    dg = SG_s[:, tt, :].rearrange("p (e c) -> p e c", c=cap) if i else SG_p[:, :, 0:cap]
                    last = dve.tensor_scalar(dst, b[:, 0:n], iota[:, tt:tt + 1], None, ALU.is_equal)
                    if tt == i:
                        x_free(last)
                        x_settle()
                    else:
                        link(last)
                    dve.tensor_tensor(dg, dst.rearrange("p (e c) -> p e c", c=cap),
                                      wide(affin[:, i + tt, :], cap), ALU.mult).then_inc(sem("SG_ready"), 1)
            for k in range(KT):
                for cnd, (cap, o) in enumerate(((CAP_P, CAP_S), (CAP_S, 0))):
                    b = x_take()
                    x_free(dve.tensor_scalar(xeT[:, k, :, o:o + cap], b[:, 0:NE * cap].rearrange("p (e c) -> p e c", c=cap),
                                             aff2[:, k, cnd:cnd + 1], aff2[:, KT + k, cnd:cnd + 1], ALU.mult, ALU.add))
                if k == KT // 2:
                    for j in range(NE // GE):
                        b = x_take()
                        x_free(dve.tensor_copy(Gt_s[:, j, :], b[:, 0:2 * P]))
                    b = x_take()
                    x_free(dve.tensor_copy(Gt_p, b[:, :].rearrange("p (j t) -> p j t", t=P)))
            x_settle()
            c.settle()
            with dve.Fori(0, NE // GE) as g:
                def hidden_to_cm(i, j):
                    dve.wait_ge(sem("hT_psum"), g * 16 + (4 * i + j + 1))
                    dve.tensor_copy(hT[:, 4 * j:4 * j + 4, :].rearrange("p (q a) s -> p a q s", a=2),
                                    psum[:, 4, 0:2 * P].rearrange("p (a q s) -> p a q s", a=2, q=2)).then_inc(sem("hT_done"), 1)

                for i in range(GE):
                    dve.tensor_copy(xe[:, :, 0:CAP], xeT[:, :, bass.ds(g * GE + i, 1), :].rearrange("p a b c -> p a (b c)"))\
                       .then_inc(sem("xe_ready"), 1)
                    if i == 0:
                        dve.tensor_copy(Gs_cur, Gt_s[:, bass.ds(g, 1), :].rearrange("p a t -> p (a t)"))
                        dve.tensor_copy(Gp_cur, Gt_p[:, bass.ds(g, 1), :].rearrange("p a t -> p (a t)"))\
                           .then_inc(sem("Gcur_ready"), 1)
                    for j in range(4):
                        dve.wait_ge(sem("sg_ready"), g * 16 + (4 * i + j + 1))
                        dve.tensor_tensor(h_sb[:, j % 2, :], sg[:, j % 2, :], psum[:, 2 + j % 2, 0:2 * P], ALU.mult)\
                           .then_inc(sem("h_done"), 1)
                        if j:
                            hidden_to_cm(i, j - 1)
                    hidden_to_cm(i, 3)
                for n, (t, half) in enumerate([(t, half) for t in range(NT) for half in range(2)]):
                    dve.wait_ge(sem("comb_ready"), g * 6 + (n + 1))
                    acc = y[:, t, half * CW:(half + 1) * CW]
                    dve.tensor_tensor(acc, acc, psum[:, (7, 4)[n % 2], :], ALU.add).then_inc(sem("comb_done"), 1)
            dve.wait_ge(sem("comb_done"), 2 + 6 * (NE // GE))
            residual(24, 20, "ms4_ready", "out_ready", 9)

    return nc


def kernel(**inputs):
    import numpy as _np
    import concourse.bacc as _bacc
    from concourse import mybir as _mybir
    from concourse.bass_utils import run_bass_kernel_spmd as _run

    names = ["x_prompt", "x_sample", "cache_k", "cache_v", "state_ssd", "c", "c_ctx", "w_ada", "b_ada",
             "g_pre_mix", "g_post_mix", "g_pre_ffn", "g_post_ffn", "w_in", "lam_q1", "lam_k1", "lam_q2", "lam_k2",
             "w_subln", "conv_w", "conv_b", "dt_bias", "a_log", "d_skip", "w_ssd_norm", "w_o_attn", "w_o_ssd",
             "w_out", "w_router", "w_gate", "w_up", "w_down"]
    nc = _bacc.Bacc("TRN2", target_bir_lowering=False, num_devices=1)
    arrays, t_in, t_out = {}, {}, {}
    f32 = _mybir.dt.float32
    for name in names:
        a = _np.ascontiguousarray(inputs[name])
        arrays["in_" + name] = a
        t_in[name] = nc.dram_tensor("in_" + name, a.shape, f32, kind="ExternalInput").ap()
    arrays["shape_consts"] = shape_constants()
    consts = nc.dram_tensor("shape_consts", (P, C_END), f32, kind="ExternalInput").ap()
    outs = {"xp": (1, P, D), "xs": (1, 2 * P, D), "k": (1, 1, P, A_HEADS, 2 * A_HD),
            "v": (1, 1, P, A_HEADS, A_VD), "state": (1, 1, 2, S_HEADS, S_HD, S_STATE)}
    for name, shape in outs.items():
        t_out[name] = nc.dram_tensor("out_" + name, shape, f32, kind="ExternalOutput").ap()
    scratch = nc.dram_tensor("cs_rows", (2, NT, S_HEADS, P), f32, kind="Internal").ap()
    build(nc, t_in, t_out, consts, scratch)
    r = _run(nc, [arrays], core_ids=[0])
    return tuple(r.results[0]["out_" + name] for name in outs)
```
